# Optimizing a Trainium2 kernel written in Bass

```python
import math
import jax, jax.numpy as jnp
from jax import lax
import numpy as np
import jax
import jax.numpy as jnp

D_MODEL = 1024
BATCH = 1
SEQ = 512
DEPTH = 2

HEAD_DIM = 128
ROT_DIM = HEAD_DIM // 4
ROPE_THETA = 500000.0
DIL_PAIRS = ((128, 1), (512, 4), (2048, 16))
N_GROUPS = len(DIL_PAIRS)
A_HEADS = D_MODEL // HEAD_DIM
A_WIDTH = A_HEADS * HEAD_DIM
A_QKV = N_GROUPS * A_WIDTH
B_HEADS = D_MODEL // HEAD_DIM
B_KEY = 128
B_VAL = 128
B_WIDTH = B_HEADS * B_VAL
CHUNK = 64
MEM_LEN = 256
MEM_HEADS = 4
MEM_WIDTH = MEM_HEADS * HEAD_DIM
MIX_WIDTH = A_WIDTH + MEM_WIDTH
IN_A = 3 * A_QKV + MEM_WIDTH + MIX_WIDTH
IN_B = 3 * B_HEADS * B_KEY + MEM_WIDTH + MIX_WIDTH
N_A_LAYERS = (DEPTH + 1) // 2
N_B_LAYERS = DEPTH // 2
EPS = 1e-6
ATTN_SCALE = 1.0 / math.sqrt(HEAD_DIM)


def rms_norm(x, g):
    xf = x.astype(jnp.float32)
    y = xf * lax.rsqrt(jnp.mean(xf * xf, axis=-1, keepdims=True) + EPS)
    return (y * g.astype(jnp.float32)).astype(x.dtype)

def rotary_tables(positions):
    inv_freq = ROPE_THETA ** (-jnp.arange(0, ROT_DIM, 2, dtype=jnp.float32) / ROT_DIM)
    ang = positions.astype(jnp.float32)[..., None] * inv_freq
    return jnp.cos(ang), jnp.sin(ang)

def apply_partial_rotary(x, cos, sin):
    xf = x.astype(jnp.float32)
    half = ROT_DIM // 2
    x1, x2, rest = xf[..., :half], xf[..., half:ROT_DIM], xf[..., ROT_DIM:]
    out = jnp.concatenate([x1 * cos - x2 * sin, x2 * cos + x1 * sin, rest], axis=-1)
    return out.astype(x.dtype)

def dilated_window_attention(q, k, v, dilation, n_back):
    B, S, H, Dh = q.shape
    span = dilation * n_back
    Sp = -(-S // span) * span
    nb = Sp // span

    def to_blocks(t):
        t = jnp.pad(t, ((0, 0), (0, Sp - S), (0, 0), (0, 0)))
        return t.reshape(B, nb, n_back, dilation, H, Dh).transpose(0, 3, 1, 2, 4, 5)

    qb, kb, vb = to_blocks(q), to_blocks(k), to_blocks(v)
    shift = lambda t: jnp.pad(t, ((0, 0), (0, 0), (1, 0), (0, 0), (0, 0), (0, 0)))[:, :, :-1]
    kc = jnp.concatenate([shift(kb), kb], axis=3)
    vc = jnp.concatenate([shift(vb), vb], axis=3)
    s = jnp.einsum('brcqhd,brckhd->brchqk', qb, kc).astype(jnp.float32) * ATTN_SCALE
    i = jnp.arange(n_back)[:, None]
    j = jnp.arange(2 * n_back)[None, :]
    dist = n_back + i - j
    band = (dist >= 0) & (dist <= n_back)
    c = jnp.arange(nb)[:, None, None]
    valid = band[None] & ((c * n_back + j[None] - n_back) >= 0)
    valid = valid[None, None, :, None]
    s = jnp.where(valid, s, -jnp.inf)
    m = jnp.max(s, axis=-1, keepdims=True)
    p = jnp.exp(s - m)
    den = jnp.sum(p, axis=-1, keepdims=True)
    o = jnp.einsum('brchqk,brckhd->brcqhd', p.astype(v.dtype), vc).astype(jnp.float32)
    o = o / jnp.moveaxis(den, 3, 4)
    lse = (m + jnp.log(den))[..., 0]
    o = o.transpose(0, 2, 3, 1, 4, 5).reshape(B, Sp, H, Dh)[:, :S]
    lse = lse.transpose(0, 2, 4, 1, 3).reshape(B, Sp, H)[:, :S]
    return o, lse

def dilated_mixer(cols, cos, sin, q_gain, k_gain):
    B, S, _ = cols.shape
    qkv = cols.reshape(B, S, 3, N_GROUPS, A_HEADS, HEAD_DIM)
    q = rms_norm(qkv[:, :, 0], q_gain[:, None, :])
    k = rms_norm(qkv[:, :, 1], k_gain[:, None, :])
    v = qkv[:, :, 2]
    cos5, sin5 = cos[:, :, None, None, :], sin[:, :, None, None, :]
    q = apply_partial_rotary(q, cos5, sin5)
    k = apply_partial_rotary(k, cos5, sin5)
    outs, lses = [], []
    for g, (window, dil) in enumerate(DIL_PAIRS):
        o, lse = dilated_window_attention(q[:, :, g], k[:, :, g], v[:, :, g], dil, window // dil)
        outs.append(o)
        lses.append(lse)
    alpha = jax.nn.softmax(jnp.stack(lses, axis=0), axis=0)
    o = jnp.sum(alpha[..., None] * jnp.stack(outs, axis=0), axis=0)
    return o.reshape(B, S, A_WIDTH).astype(cols.dtype)

def gla_chunk_scan(q, k, v, log_f):
    B, S, H, dk = q.shape
    dv = v.shape[-1]
    nc = S // CHUNK
    to_c = lambda t: t.reshape(B, nc, CHUNK, H, t.shape[-1]).transpose(1, 0, 3, 2, 4)
    qc, kc, vc = to_c(q), to_c(k), to_c(v)
    G = jnp.cumsum(to_c(log_f), axis=3)
    causal = jnp.tril(jnp.ones((CHUNK, CHUNK), dtype=bool))[..., None]

    def step(state, inp):
        qt, kt, vt, Gt = inp
        o_inter = jnp.einsum('bhtk,bhkv->bhtv', qt * jnp.exp(Gt), state)
        diff = Gt[:, :, :, None, :] - Gt[:, :, None, :, :]
        decay = jnp.where(causal, jnp.exp(jnp.where(causal, diff, 0.0)), 0.0)
        attn = jnp.einsum('bhtk,bhsk,bhtsk->bhts', qt, kt, decay)
        o_intra = jnp.einsum('bhts,bhsv->bhtv', attn, vt)
        g_last = Gt[:, :, -1:, :]
        k_dec = kt * jnp.exp(g_last - Gt)
        new_state = jnp.exp(g_last[:, :, 0, :])[..., None] * state + jnp.einsum('bhsk,bhsv->bhkv', k_dec, vt)
        return new_state, o_inter + o_intra

    init = jnp.zeros((B, H, dk, dv), jnp.float32)
    _, o = lax.scan(step, init, (qc, kc, vc, G))
    return o.transpose(1, 0, 3, 2, 4).reshape(B, S, H, dv)

def hgrn2_mixer(cols, lb, o_gain):
    B, S, _ = cols.shape
    w = B_HEADS * B_KEY
    q = cols[..., :w].astype(jnp.float32)
    f = cols[..., w:2 * w].astype(jnp.float32)
    iv = cols[..., 2 * w:].astype(jnp.float32)
    log_f = jnp.logaddexp(jnp.log(lb), jnp.log1p(-lb) + jax.nn.log_sigmoid(f))
    k = (1.0 - lb) * jax.nn.sigmoid(-f)
    sh = lambda t, d: t.reshape(B, S, B_HEADS, d)
    o = gla_chunk_scan(sh(q, B_KEY), sh(k, B_KEY), sh(iv, B_VAL), sh(log_f, B_KEY))
    o = rms_norm(o, o_gain)
    return o.reshape(B, S, B_WIDTH).astype(cols.dtype)

def memory_cross_attention(q_cols, mem, mem_gain, w_kv, q_gain, k_gain):
    B, S, _ = q_cols.shape
    M = mem.shape[1]
    kv = rms_norm(mem, mem_gain) @ w_kv
    km = rms_norm(kv[..., :MEM_WIDTH].reshape(B, M, MEM_HEADS, HEAD_DIM), k_gain)
    vm = kv[..., MEM_WIDTH:].reshape(B, M, MEM_HEADS, HEAD_DIM)
    qm = rms_norm(q_cols.reshape(B, S, MEM_HEADS, HEAD_DIM), q_gain)
    s = jnp.einsum('bshd,bmhd->bhsm', qm, km).astype(jnp.float32) * ATTN_SCALE
    p = jax.nn.softmax(s, axis=-1)
    o = jnp.einsum('bhsm,bmhd->bshd', p.astype(vm.dtype), vm)
    return o.reshape(B, S, MEM_WIDTH)

def first_inputs(seed: int = 0) -> dict:
    key = jax.random.key(seed)
    ks = jax.random.split(key, 16)
    nrm = lambda k, shape, scale: jax.random.normal(k, shape, jnp.float32) * scale
    gain = lambda k, shape: 1.0 + 0.05 * jax.random.normal(k, shape, jnp.float32)
    x = nrm(ks[0], (BATCH, SEQ, D_MODEL), 1.0)
    mem = nrm(ks[1], (BATCH, MEM_LEN, D_MODEL), 1.0)
    offsets = jax.random.randint(ks[2], (BATCH, 1), 0, 4096, dtype=jnp.int32)
    positions = offsets + jnp.arange(SEQ, dtype=jnp.int32)[None, :]
    return {
        "x": x,
        "mem": mem,
        "positions": positions,
        "norm_gain": gain(ks[3], (DEPTH, D_MODEL)),
        "w_in_a": nrm(ks[4], (N_A_LAYERS, D_MODEL, IN_A), D_MODEL ** -0.5),
        "q_gain_a": gain(ks[5], (N_A_LAYERS, N_GROUPS, HEAD_DIM)),
        "k_gain_a": gain(ks[6], (N_A_LAYERS, N_GROUPS, HEAD_DIM)),
        "w_out_a": nrm(ks[7], (N_A_LAYERS, MIX_WIDTH, D_MODEL), MIX_WIDTH ** -0.5),
        "w_in_b": nrm(ks[8], (N_B_LAYERS, D_MODEL, IN_B), D_MODEL ** -0.5),
        "lb_logits": nrm(ks[9], (DEPTH, B_HEADS * B_KEY), 0.5),
        "o_gain_b": gain(ks[10], (N_B_LAYERS, B_VAL)),
        "w_out_b": nrm(ks[11], (N_B_LAYERS, MIX_WIDTH, D_MODEL), MIX_WIDTH ** -0.5),
        "mem_norm_gain": gain(ks[12], (DEPTH, D_MODEL)),
        "w_mem_kv": nrm(ks[13], (DEPTH, D_MODEL, 2 * MEM_WIDTH), D_MODEL ** -0.5),
        "mem_q_gain": gain(ks[14], (DEPTH, HEAD_DIM)),
        "mem_k_gain": gain(ks[15], (DEPTH, HEAD_DIM)),
    }

def first_block(x, mem, positions, norm_gain, w_in_a, q_gain_a, k_gain_a, w_out_a,
              w_in_b, lb_logits, o_gain_b, w_out_b, mem_norm_gain, w_mem_kv,
              mem_q_gain, mem_k_gain):
    cos, sin = rotary_tables(positions)
    sm = jax.nn.softmax(lb_logits.astype(jnp.float32), axis=0)
    lower_bounds = jnp.cumsum(sm, axis=0) - sm[0:1]
    for l in range(DEPTH):
        j = l // 2
        h = rms_norm(x, norm_gain[l])
        if l % 2 == 0:
            cols = h @ w_in_a[j]
            mix = dilated_mixer(cols[..., :3 * A_QKV], cos, sin, q_gain_a[j], k_gain_a[j])
            q_mem = cols[..., 3 * A_QKV:3 * A_QKV + MEM_WIDTH]
            gate = cols[..., 3 * A_QKV + MEM_WIDTH:]
            w_out = w_out_a[j]
        else:
            cols = h @ w_in_b[j]
            wb = 3 * B_HEADS * B_KEY
            mix = hgrn2_mixer(cols[..., :wb], lower_bounds[l], o_gain_b[j])
            q_mem = cols[..., wb:wb + MEM_WIDTH]
            gate = cols[..., wb + MEM_WIDTH:]
            w_out = w_out_b[j]
        mem_out = memory_cross_attention(q_mem, mem, mem_norm_gain[l], w_mem_kv[l],
                                         mem_q_gain[l], mem_k_gain[l])
        y = jnp.concatenate([mix, mem_out], axis=-1) * jax.nn.silu(gate)
        x = x + y @ w_out
    return x


GRID_W = 64
CTX_LEN = 256
HEAD_DIM_2 = 64
ROPE_BASE = 10000.0
NORM_EPS = 1e-6
NEG_INF = -1e30
Q_BLOCK = 128
DIFF_HEADS = 4
DIFF_WIDTH = DIFF_HEADS * 2 * HEAD_DIM_2
NA_HEADS = 8
NA_WIDTH = NA_HEADS * HEAD_DIM_2
NA_MAX_ROWS = 8
NA_COLS = 16
AB_Q_COLS = DIFF_WIDTH + NA_WIDTH
AB_IN = 3 * DIFF_WIDTH + 3 * NA_WIDTH
AB_OUT = DIFF_WIDTH + NA_WIDTH
GQA_HEADS = 16
GQA_KV_HEADS = 4
GQA_GROUP = GQA_HEADS // GQA_KV_HEADS
SWA_WINDOW = 128
C_Q_COLS = GQA_HEADS * HEAD_DIM_2
C_KV_COLS = GQA_KV_HEADS * HEAD_DIM_2
C_IN = C_Q_COLS + 2 * C_KV_COLS
FFN_HIDDEN = (8 * D_MODEL + 3 * 256 - 1) // (3 * 256) * 256
N_EVEN = (DEPTH + 1) // 2
N_ODD = DEPTH // 2


def rmsnorm(x, g):
    xf = x.astype(jnp.float32)
    y = xf * lax.rsqrt(jnp.mean(xf * xf, axis=-1, keepdims=True) + NORM_EPS)
    return (y * g.astype(jnp.float32)).astype(x.dtype)

def modulate(h, shift, scale):
    return h * (1 + scale) + shift

def swiglu(h, w1, w3, w2):
    return (jax.nn.silu(h @ w1) * (h @ w3)) @ w2

def axial_rope_tables(n, dtype):
    t = jnp.arange(n)
    row = (t // GRID_W).astype(jnp.float32)
    col = (t % GRID_W).astype(jnp.float32)
    quarter = HEAD_DIM_2 // 4
    inv = ROPE_BASE ** (-jnp.arange(quarter, dtype=jnp.float32) / quarter)
    ar = row[:, None] * inv
    ac = col[:, None] * inv
    ang = jnp.concatenate([ar, ar, ac, ac], axis=-1)
    return jnp.cos(ang).astype(dtype), jnp.sin(ang).astype(dtype)

def apply_rope(x, cos, sin):
    xs = x.reshape(x.shape[:-1] + (2, 2, HEAD_DIM_2 // 4))
    rot = jnp.stack([-xs[..., 1, :], xs[..., 0, :]], axis=-2).reshape(x.shape)
    return x * cos[None, :, None, :] + rot * sin[None, :, None, :]

def heads(t, n_heads):
    return t.reshape(t.shape[:2] + (n_heads, -1))

def block_sweep(fn, q):
    B, S = q.shape[:2]
    nb = S // Q_BLOCK
    qb = jnp.moveaxis(q.reshape((B, nb, Q_BLOCK) + q.shape[2:]), 1, 0)
    starts = jnp.arange(nb) * Q_BLOCK
    out = lax.map(lambda a: fn(a[0], a[1]), (qb, starts))
    return jnp.moveaxis(out, 0, 1).reshape((B, S) + out.shape[3:])

def plain_attention(q, k, v):
    s = jnp.einsum('bqhd,bnhd->bhqn', q, k).astype(jnp.float32) * (HEAD_DIM_2 ** -0.5)
    p = jax.nn.softmax(s, axis=-1).astype(v.dtype)
    return jnp.einsum('bhqn,bnhd->bqhd', p, v)

def diff_attend(q, k, v, lam_val):
    B, Q = q.shape[:2]
    s = jnp.einsum('bqhd,bnhd->bhqn', q, k).astype(jnp.float32) * (HEAD_DIM_2 ** -0.5)
    p = jax.nn.softmax(s, axis=-1).reshape(B, DIFF_HEADS, 2, Q, -1)
    p = p[:, :, 0] - lam_val * p[:, :, 1]
    return jnp.einsum('bhqn,bnhd->bqhd', p.astype(v.dtype), v)

def diff_out(a, sub_g, lam_init):
    return (rmsnorm(a, sub_g) * (1.0 - lam_init)).reshape(a.shape[:2] + (-1,))

def neighbourhood_attention(q, k, v, k_c, v_c, rpb):
    B, S, _ = q.shape
    rows = S // GRID_W
    kr = min(NA_MAX_ROWS, rows)
    kc = NA_COLS
    grid = lambda t: t.reshape(B, rows, GRID_W, NA_HEADS, HEAD_DIM_2)
    qg, kg, vg = grid(q), grid(k), grid(v)
    kcx, vcx = heads(k_c, NA_HEADS), heads(v_c, NA_HEADS)
    col = jnp.arange(GRID_W)
    col_start = jnp.clip(col - kc // 2, 0, GRID_W - kc)
    col_idx = col_start[:, None] + jnp.arange(kc)
    dc_idx = col_idx - col[:, None] + (NA_COLS - 1)
    rpb_cols = rpb[:, :, dc_idx]
    scale = HEAD_DIM_2 ** -0.5

    def row_fn(args):
        q_r, r = args
        rs = jnp.clip(r - kr // 2, 0, rows - kr)
        k_r = lax.dynamic_slice_in_dim(kg, rs, kr, axis=1)[:, :, col_idx]
        v_r = lax.dynamic_slice_in_dim(vg, rs, kr, axis=1)[:, :, col_idx]
        dr_idx = rs + jnp.arange(kr) - r + (NA_MAX_ROWS - 1)
        bias = jnp.transpose(rpb_cols[:, dr_idx], (0, 2, 1, 3))
        s_nb = jnp.einsum('bchd,bicjhd->bhcij', q_r, k_r).astype(jnp.float32) * scale + bias
        s_ctx = jnp.einsum('bchd,bnhd->bhcn', q_r, kcx).astype(jnp.float32) * scale
        s = jnp.concatenate([s_nb.reshape(B, NA_HEADS, GRID_W, kr * kc), s_ctx], axis=-1)
        p = jax.nn.softmax(s, axis=-1).astype(v.dtype)
        p_nb = p[..., :kr * kc].reshape(B, NA_HEADS, GRID_W, kr, kc)
        p_ctx = p[..., kr * kc:]
        return (jnp.einsum('bhcij,bicjhd->bchd', p_nb, v_r)
                + jnp.einsum('bhcn,bnhd->bchd', p_ctx, vcx))

    out = lax.map(row_fn, (jnp.moveaxis(qg, 1, 0), jnp.arange(rows)))
    return jnp.moveaxis(out, 0, 1).reshape(B, S, NA_WIDTH)

def mixer_ab(h_x, h_c, w_in, w_out, lam, sub_g, rpb, lam_init, cos, sin, with_ctx_out):
    B, S, _ = h_x.shape
    n_c = h_c.shape[1]
    cuts = [DIFF_WIDTH, AB_Q_COLS, AB_Q_COLS + DIFF_WIDTH, AB_Q_COLS + 2 * DIFF_WIDTH,
            AB_Q_COLS + 2 * DIFF_WIDTH + NA_WIDTH]
    aq_x, bq_x, ak_x, av_x, bk_x, bv_x = jnp.split(h_x @ w_in, cuts, axis=-1)
    if with_ctx_out:
        p_c = h_c @ w_in
        aq_c, bq_c, kv_c = p_c[..., :DIFF_WIDTH], p_c[..., DIFF_WIDTH:AB_Q_COLS], p_c[..., AB_Q_COLS:]
    else:
        kv_c = h_c @ w_in[:, AB_Q_COLS:]
    ak_c, av_c, bk_c, bv_c = jnp.split(kv_c, [DIFF_WIDTH, 2 * DIFF_WIDTH, 2 * DIFF_WIDTH + NA_WIDTH], axis=-1)

    lf = lam.astype(jnp.float32)
    lam_val = jnp.exp(jnp.sum(lf[0] * lf[1])) - jnp.exp(jnp.sum(lf[2] * lf[3])) + lam_init
    aq_xh = apply_rope(heads(aq_x, 2 * DIFF_HEADS), cos, sin)
    ak_xh = apply_rope(heads(ak_x, 2 * DIFF_HEADS), cos, sin)
    ak_ch, av_ch = heads(ak_c, 2 * DIFF_HEADS), heads(av_c, DIFF_HEADS)
    k_all = jnp.concatenate([ak_ch, ak_xh], axis=1)
    v_all = jnp.concatenate([av_ch, heads(av_x, DIFF_HEADS)], axis=1)
    a_x = block_sweep(lambda qb, start: diff_attend(qb, k_all, v_all, lam_val), aq_xh)
    a_x = diff_out(a_x, sub_g, lam_init)

    b_x = neighbourhood_attention(bq_x, bk_x, bv_x, bk_c, bv_c, rpb)
    out_x = jnp.concatenate([a_x, b_x], axis=-1) @ w_out

    out_c = None
    if with_ctx_out:
        a_c = diff_out(diff_attend(heads(aq_c, 2 * DIFF_HEADS), ak_ch, av_ch, lam_val), sub_g, lam_init)
        b_c = plain_attention(heads(bq_c, NA_HEADS), heads(bk_c, NA_HEADS),
                              heads(bv_c, NA_HEADS)).reshape(B, n_c, NA_WIDTH)
        out_c = jnp.concatenate([a_c, b_c], axis=-1) @ w_out
    return out_x, out_c

def gqa_sink_attend(q, k, v, mask, sinks):
    B, Q = q.shape[:2]
    qg = q.reshape(B, Q, GQA_KV_HEADS, GQA_GROUP, HEAD_DIM_2)
    s = jnp.einsum('bqkgd,bnkd->bkgqn', qg, k).astype(jnp.float32) * (HEAD_DIM_2 ** -0.5)
    if mask is not None:
        s = jnp.where(mask, s, NEG_INF)
    sink = jnp.broadcast_to(sinks.astype(jnp.float32).reshape(GQA_KV_HEADS, GQA_GROUP, 1, 1),
                            (B, GQA_KV_HEADS, GQA_GROUP, Q, 1))
    p = jax.nn.softmax(jnp.concatenate([s, sink], axis=-1), axis=-1)[..., :-1]
    o = jnp.einsum('bkgqn,bnkd->bqkgd', p.astype(v.dtype), v)
    return o.reshape(B, Q, GQA_HEADS, HEAD_DIM_2)

def mixer_c(h_x, h_c, w_in, w_out, sinks, cos, sin, with_ctx_out):
    B, S, _ = h_x.shape
    q_x, k_x, v_x = jnp.split(h_x @ w_in, [C_Q_COLS, C_Q_COLS + C_KV_COLS], axis=-1)
    q_x = apply_rope(heads(q_x, GQA_HEADS), cos, sin)
    k_x = apply_rope(heads(k_x, GQA_KV_HEADS), cos, sin)
    v_x = heads(v_x, GQA_KV_HEADS)
    if with_ctx_out:
        p_c = h_c @ w_in
        q_c, kv_c = p_c[..., :C_Q_COLS], p_c[..., C_Q_COLS:]
    else:
        kv_c = h_c @ w_in[:, C_Q_COLS:]
    k_c, v_c = jnp.split(kv_c, 2, axis=-1)
    k_c, v_c = heads(k_c, GQA_KV_HEADS), heads(v_c, GQA_KV_HEADS)
    n_c = k_c.shape[1]

    pad = ((0, 0), (SWA_WINDOW, SWA_WINDOW), (0, 0), (0, 0))
    k_pad, v_pad = jnp.pad(k_x, pad), jnp.pad(v_x, pad)
    span = Q_BLOCK + 2 * SWA_WINDOW
    ctx_mask = jnp.ones((Q_BLOCK, n_c), dtype=bool)

    def blk(q_b, start):
        k_b = lax.dynamic_slice_in_dim(k_pad, start, span, axis=1)
        v_b = lax.dynamic_slice_in_dim(v_pad, start, span, axis=1)
        q_pos = start + jnp.arange(Q_BLOCK)
        k_pos = start - SWA_WINDOW + jnp.arange(span)
        band = ((k_pos >= 0) & (k_pos < S))[None, :] & (jnp.abs(q_pos[:, None] - k_pos[None, :]) <= SWA_WINDOW)
        return gqa_sink_attend(q_b, jnp.concatenate([k_c, k_b], axis=1),
                               jnp.concatenate([v_c, v_b], axis=1),
                               jnp.concatenate([ctx_mask, band], axis=-1), sinks)

    out_x = block_sweep(blk, q_x).reshape(B, S, C_Q_COLS) @ w_out
    out_c = None
    if with_ctx_out:
        o_c = gqa_sink_attend(heads(q_c, GQA_HEADS), k_c, v_c, None, sinks)
        out_c = o_c.reshape(B, n_c, C_Q_COLS) @ w_out
    return out_x, out_c

def second_inputs(seed: int = 0) -> dict:
    key = jax.random.key(seed)
    ks = jax.random.split(key, 19)
    nrm = lambda k, shape, std: jax.random.normal(k, shape, jnp.float32) * std
    D = D_MODEL
    return {
        'x': nrm(ks[0], (BATCH, SEQ, D), 1.0),
        'c': nrm(ks[1], (BATCH, D), 1.0),
        'ctx': nrm(ks[2], (BATCH, CTX_LEN, D), 1.0),
        'c_ctx': nrm(ks[3], (D,), 1.0),
        'ada_w': nrm(ks[4], (DEPTH, D, 6 * D), 0.5 * D ** -0.5),
        'ada_b': nrm(ks[5], (DEPTH, 6 * D), 0.02),
        'norm_g': 1.0 + nrm(ks[6], (DEPTH, 2, D), 0.01),
        'w_in_ab': nrm(ks[7], (N_EVEN, D, AB_IN), D ** -0.5),
        'w_out_ab': nrm(ks[8], (N_EVEN, AB_OUT, D), AB_OUT ** -0.5),
        'diff_lambda': nrm(ks[9], (N_EVEN, 4, HEAD_DIM_2), 0.1),
        'diff_sub_g': 1.0 + nrm(ks[10], (N_EVEN, 2 * HEAD_DIM_2), 0.01),
        'na_rpb': nrm(ks[11], (N_EVEN, NA_HEADS, 2 * NA_MAX_ROWS - 1, 2 * NA_COLS - 1), 0.1),
        'w_in_c': nrm(ks[12], (N_ODD, D, C_IN), D ** -0.5),
        'w_out_c': nrm(ks[13], (N_ODD, C_Q_COLS, D), C_Q_COLS ** -0.5),
        'attn_sinks': nrm(ks[14], (N_ODD, GQA_HEADS), 0.5),
        'ffn_w1': nrm(ks[15], (DEPTH, D, FFN_HIDDEN), D ** -0.5),
        'ffn_w3': nrm(ks[16], (DEPTH, D, FFN_HIDDEN), D ** -0.5),
        'ffn_w2': nrm(ks[17], (DEPTH, FFN_HIDDEN, D), FFN_HIDDEN ** -0.5),
        'final_g': 1.0 + nrm(ks[18], (D,), 0.01),
    }

def second_block(x, c, ctx, c_ctx, ada_w, ada_b, norm_g, w_in_ab, w_out_ab, diff_lambda, diff_sub_g,
              na_rpb, w_in_c, w_out_c, attn_sinks, ffn_w1, ffn_w3, ffn_w2, final_g):
    B, S, _ = x.shape
    cos, sin = axial_rope_tables(S, x.dtype)
    for layer in range(DEPTH):
        ctx_out = layer < DEPTH - 1
        mod_x = jnp.split((jax.nn.silu(c) @ ada_w[layer] + ada_b[layer])[:, None, :], 6, axis=-1)
        mod_c = jnp.split(jax.nn.silu(c_ctx) @ ada_w[layer] + ada_b[layer], 6, axis=-1)
        h_x = modulate(rmsnorm(x, norm_g[layer, 0]), mod_x[0], mod_x[1])
        h_c = modulate(rmsnorm(ctx, norm_g[layer, 0]), mod_c[0], mod_c[1])
        if layer % 2 == 0:
            e = layer // 2
            lam_init = 0.8 - 0.6 * math.exp(-0.3 * layer)
            o_x, o_c = mixer_ab(h_x, h_c, w_in_ab[e], w_out_ab[e], diff_lambda[e], diff_sub_g[e],
                                na_rpb[e], lam_init, cos, sin, ctx_out)
        else:
            o = layer // 2
            o_x, o_c = mixer_c(h_x, h_c, w_in_c[o], w_out_c[o], attn_sinks[o], cos, sin, ctx_out)
        x = x + mod_x[2] * o_x
        h_x = modulate(rmsnorm(x, norm_g[layer, 1]), mod_x[3], mod_x[4])
        x = x + mod_x[5] * swiglu(h_x, ffn_w1[layer], ffn_w3[layer], ffn_w2[layer])
        if ctx_out:
            ctx = ctx + mod_c[2] * o_c
            h_c = modulate(rmsnorm(ctx, norm_g[layer, 1]), mod_c[3], mod_c[4])
            ctx = ctx + mod_c[5] * swiglu(h_c, ffn_w1[layer], ffn_w3[layer], ffn_w2[layer])
    return rmsnorm(x, final_g)


def setup_inputs(seed=0):
    out = dict(first_inputs(seed))
    for name, value in second_inputs(seed + 1).items():
        if name != "x":
            out[name + "_2"] = value
    return out


def reference(
    x, mem, positions, norm_gain, w_in_a, q_gain_a, k_gain_a, w_out_a, w_in_b, lb_logits,
    o_gain_b, w_out_b, mem_norm_gain, w_mem_kv, mem_q_gain, mem_k_gain, c_2, ctx_2, c_ctx_2,
    ada_w_2, ada_b_2, norm_g_2, w_in_ab_2, w_out_ab_2, diff_lambda_2, diff_sub_g_2, na_rpb_2,
    w_in_c_2, w_out_c_2, attn_sinks_2, ffn_w1_2, ffn_w3_2, ffn_w2_2, final_g_2,
):
    x = first_block(
        x, mem, positions, norm_gain, w_in_a, q_gain_a, k_gain_a, w_out_a, w_in_b, lb_logits,
        o_gain_b, w_out_b, mem_norm_gain, w_mem_kv, mem_q_gain, mem_k_gain,
    )
    return second_block(
        x, c_2, ctx_2, c_ctx_2, ada_w_2, ada_b_2, norm_g_2, w_in_ab_2, w_out_ab_2,
        diff_lambda_2, diff_sub_g_2, na_rpb_2, w_in_c_2, w_out_c_2, attn_sinks_2, ffn_w1_2,
        ffn_w3_2, ffn_w2_2, final_g_2,
    )


_drawn_inputs = setup_inputs


def setup_inputs(seed=0):
    import zlib

    import numpy as np

    out = dict(_drawn_inputs(seed))
    spreads = {}
    factors = {'q_gain_a': 8.0,
     'k_gain_a': 8.0,
     'mem_norm_gain': 8.0,
     'mem_q_gain': 8.0,
     'mem_k_gain': 8.0,
     'norm_g_2': 8.0,
     'diff_lambda_2': 23.491,
     'diff_sub_g_2': 31.535,
     'na_rpb_2': 8.0,
     'attn_sinks_2': 8.0,
     'final_g_2': 32.052}
    for name, (base, spread) in spreads.items():
        noise = np.random.default_rng([zlib.crc32(name.encode()), seed]).standard_normal(out[name].shape)
        drawn = base * np.exp(spread * noise) if base else spread * noise
        out[name] = jnp.asarray(drawn.astype(out[name].dtype))
    for name, factor in factors.items():
        out[name] = (out[name] * factor).astype(out[name].dtype)
    return out
```

```python
import contextlib
import math

import numpy as np
import concourse.bass as bass
from concourse import mybir

F32 = mybir.dt.float32
F32R = mybir.dt.float32r
BF16 = mybir.dt.bfloat16
I32 = mybir.dt.int32
ALU = mybir.AluOpType
ACT = mybir.ActivationFunctionType
AX = mybir.AxisListType

P = 128
D = 1024
KD = D // P
S = 512
NT = S // P
CTX = 256
NC = CTX // P
HD = 128
AH = 8
NG = 3
DILS = (1, 4, 16)
BACK = 128
ROT = 32
HALF = ROT // 2
MH = 4
MEMW = MH * HD
MIX = AH * HD + MEMW
HD2 = 64
GRID_W = 64
NA_R = 8
NA_C = 16
FFN = 2816
KF = FFN // P
NEG = -1e30
EPS = 1e-6
CHUNK = 128
LEVELS = (64, 32, 16, 8, 4, 2, 1)
SLAB = 3072
PIECE = 1536
RES = 4


def shape_constants():
    c = {}
    c["ident"] = np.eye(P, dtype=np.float32)
    pos = np.arange(S).reshape(P, RES).T
    mask = np.zeros((P, RES, 768), np.float32)
    for r in range(RES):
        q = pos[r][:, None]
        k0 = pos.reshape(-1)[None, :]
        kr = pos[r][None, :]
        for sl, k, dil in ((slice(0, 512), k0, 1), (slice(512, 640), kr, 4), (slice(640, 768), kr, 16)):
            dist = q - k
            ok = (dist >= 0) & (dist <= dil * BACK) & (dist % dil == 0)
            mask[:, r, sl] = np.where(ok, 0.0, NEG)
    c["mask_a"] = mask.reshape(P, RES * 768)
    inv = (np.float32(500000.0) ** (-np.arange(0, ROT, 2, dtype=np.float32) / np.float32(ROT))).astype(np.float32)
    c["inv_freq"] = np.broadcast_to(inv, (P, HALF)).copy()
    carry = np.ones((P, S), np.float32)
    carry[:, ::CHUNK] = 0.0
    c["carry"] = carry
    lm = np.zeros((P, 8, P), np.float32)
    s_, t_ = np.arange(P)[:, None], np.arange(P)[None, :]
    for n, L in enumerate(LEVELS):
        lm[:, n] = (s_ // (2 * L) == t_ // (2 * L)) & ((s_ // L) % 2 == 0) & ((t_ // L) % 2 == 1)
    lm[:, 7] = s_ == t_
    c["level_mask"] = lm.reshape(P, 1024)
    t = np.arange(S)
    quarter = HD2 // 4
    invq = (np.float32(10000.0) ** (-np.arange(quarter, dtype=np.float32) / np.float32(quarter))).astype(np.float32)
    ar = (t // GRID_W).astype(np.float32)[:, None] * invq
    ac = (t % GRID_W).astype(np.float32)[:, None] * invq
    ang = np.concatenate([ar, ar, ac, ac], -1)
    sign = np.tile(np.repeat(np.array([-1.0, 1.0], np.float32), quarter), 2)
    c["cos2"] = np.cos(ang).astype(np.float32)
    c["sin2"] = (np.sin(ang).astype(np.float32) * sign).astype(np.float32)
    i_, j_ = np.arange(P)[:, None], np.arange(P)[None, :]
    c["band"] = np.concatenate([np.where(j_ >= i_, 0.0, NEG), np.where(j_ <= i_, 0.0, NEG)], 1).astype(np.float32)
    return c


def bias_table(rpb):
    col = np.arange(GRID_W)
    start = np.clip(col - NA_C // 2, 0, GRID_W - NA_C)
    kc = col[None, :]
    ok = (kc >= start[:, None]) & (kc < start[:, None] + NA_C)
    dc = np.clip(kc - col[:, None] + NA_C - 1, 0, 2 * NA_C - 2)
    wide = rpb[:, :, dc]
    wide = np.where(ok[None, None], wide, np.float32(NEG)).astype(rpb.dtype)
    wide = wide.transpose(0, 2, 1, 3)
    return np.ascontiguousarray(np.concatenate([wide[:, :, 1:15], wide[:, :, 0:14]], axis=1))


class Noted:

    def matmul(self, *a, **k):
        return lambda e: e.matmul(*a, **k)

    def transpose(self, *a, **k):
        return lambda e: e.transpose(*a, **k)

    def activation(self, *a, **k):
        return lambda e: e.activation(*a, **k)

    def tensor_tensor(self, *a, **k):
        return lambda e: e.tensor_tensor(*a, **k)

    def tensor_scalar(self, *a, **k):
        return lambda e: e.tensor_scalar(*a, **k)

    def scalar_tensor_tensor(self, *a, **k):
        return lambda e: e.scalar_tensor_tensor(*a, **k)

    def tensor_copy(self, *a, **k):
        return lambda e: e.tensor_copy(*a, **k)

    def tensor_reduce(self, *a, **k):
        return lambda e: e.tensor_reduce(*a, **k)

    def reduce_max(self, *a, **k):
        return lambda e: e.reduce_max(*a, **k)

    def reciprocal(self, *a, **k):
        return lambda e: e.reciprocal(*a, **k)

    def memset(self, *a, **k):
        return lambda e: e.memset(*a, **k)

    def tensor_tensor_scan(self, *a, **k):
        return lambda e: e.tensor_tensor_scan(*a, **k)


NOTED = Noted()


class Engine:

    def __init__(self, sem):
        self.sem, self.n, self.queue, self.waited = sem, 0, [], {}

    def wait(self, *tokens):
        for t in tokens:
            if t is None:
                continue
            if isinstance(t, list):
                self.wait(*t)
                continue
            sem, value = t
            if value > self.waited.get(sem.name, 0):
                self.waited[sem.name] = value
                self.queue.append(lambda e, s=sem, v=value: e.wait_ge(s, v))

    def __call__(self, fn, *after, signal=True):
        self.wait(*after)
        issue = fn(NOTED)
        if not signal:
            self.queue.append(issue)
            return None
        self.n += 1
        self.queue.append(lambda e: issue(e).then_inc(self.sem, 1))
        return (self.sem, self.n)

    def last(self):
        return (self.sem, self.n) if self.n else None

    def emit(self, e):
        for fn in self.queue:
            fn(e)


class Dma:

    def __init__(self, sem):
        self.sem, self.n = sem, 0

    def token(self):
        return (self.sem, self.n)


def weave(main, side, ratio=1):
    live_m = live_s = True
    while live_m or live_s:
        if live_m:
            live_m = next(main, "end") != "end"
        for _ in range(ratio):
            if live_s:
                live_s = next(side, "end") != "end"


def build(nc, A, out, stage=99, debug=None):
    ctx = contextlib.ExitStack()
    sem = lambda n: ctx.enter_context(nc.semaphore(n))
    sb_in = lambda stack, n, shape, dt=F32: stack.enter_context(nc.sbuf_tensor(n, shape, dt))
    sb = lambda n, shape, dt=F32: sb_in(ctx, n, shape, dt)

    pe, act, dve, pool, sp = (Engine(sem(f"s_{n}")) for n in ("pe", "act", "dve", "pool", "sp"))

    def load(dst, src, dma, *after, eng=None):
        eng = eng or sp
        eng.wait(*after)
        dma.n += 16
        eng.queue.append(lambda e, s=dma.sem: e.dma_start(dst, src).then_inc(s, 16))
        return dma.token()

    x = sb("x", [P, NT, D])
    ctxr = None
    slab_hi = [sb(f"slab_hi{i}", [P, SLAB], F32R) for i in range(2)]
    slab_lo = [sb(f"slab_lo{i}", [P, SLAB], F32R) for i in range(2)]
    raw = [sb(f"raw{i}", [P, PIECE]) for i in range(3)]
    hx_hi = sb("hx_hi", [P, KD, S], F32R)
    hx_lo = sb("hx_lo", [P, KD, S], F32R)
    ident = sb("ident", [P, P])
    identb = sb("identb", [P, P], BF16)
    ones = sb("ones", [P, P])
    stat = sb("stat", [P, 256])
    gcol = sb("gcol", [P, 6, KD])
    gmem = sb("gmem", [P, 4, HD])
    psum = lambda n, shape: ctx.enter_context(nc.psum_tensor(n, shape, F32))
    proj_ps = [psum(f"proj{i}", [P, 512]) for i in range(3)]
    score_ps = psum("scores", [P, 1024])
    tr_ps = [psum(f"tr{i}", [P, 512]) for i in range(2)]
    out_ps = psum("outp", [P, 512])
    free = {}
    turn = {"proj": 0, "tr": 0, "stat": 0}

    def take_proj():
        i = turn["proj"] % 3
        turn["proj"] += 1
        return proj_ps[i], ("proj", i)

    def take_tr():
        i = turn["tr"] % 2
        turn["tr"] += 1
        return tr_ps[i], ("tr", i)

    def stats(n):
        if turn["stat"] + n > 256:
            turn["stat"] = 0
        a = turn["stat"]
        turn["stat"] += n
        return stat[:, a:a + n]

    s_const = Dma(sem("d_const"))
    s_raw = [Dma(sem(f"d_raw{i}")) for i in range(3)]
    s_x = Dma(sem("d_x"))
    s_misc = [Dma(sem(f"d_misc{i}")) for i in range(8)]
    s_bias = [Dma(sem(f"d_bias{i}")) for i in range(2)]
    s_out = Dma(sem("d_out"))

    jobs = []

    def job(name, K, N, segments, per=None):
        per = per or max(1, PIECE // N)
        pieces = []
        for k0 in range(0, K, per):
            k1 = min(K, k0 + per)
            pieces.append((k0, k1, [(c, w, src[k0 * P:k1 * P, :].rearrange("(k p) n -> p k n", p=P))
                                    for c, w, src in segments]))
        jobs.append((name, K, N, pieces))

    wa, wb = A["w_in_a"][0], A["w_in_b"][0]
    AQ = NG * AH * HD
    for h in range(AH):
        for g in range(NG):
            job("a", KD, 384, [(t * 128, 128, wa[:, t * AQ + (g * AH + h) * HD:][:, 0:128]) for t in range(3)])

    def mem_and_out_jobs(layer, w, base, w_out):
        kv = A["w_mem_kv"][layer]
        for m in range(MH):
            job("mkv", KD, 256, [(0, 128, kv[:, m * HD:(m + 1) * HD]), (128, 128, kv[:, MEMW + m * HD:MEMW + (m + 1) * HD])])
        job("mq", KD, 256, [(0, 256, w[:, base:base + 256])])
        job("mq", KD, 256, [(0, 256, w[:, base + 256:base + 512])])
        for n in range(MIX // 384):
            job("gate", KD, 384, [(0, 384, w[:, base + MEMW + n * 384:base + MEMW + (n + 1) * 384])])
        for n in range(4):
            job("out", MIX // P, 256, [(0, 256, w_out[:, n * 256:(n + 1) * 256])])

    mem_and_out_jobs(0, wa, 3 * AQ, A["w_out_a"][0])
    for h in range(AH):
        job("b", KD, 384, [(t * 128, 128, wb[:, t * D + h * HD:t * D + (h + 1) * HD]) for t in range(3)])
    mem_and_out_jobs(1, wb, 3 * D, A["w_out_b"][0])
    DIFF_W = 512

    def ada_jobs(layer):
        for n in range(32):
            job("ada", KD, 192, [(0, 192, A["ada_w_2"][layer][:, n * 192:(n + 1) * 192])], per=KD)

    ada_jobs(0)
    wab = A["w_in_ab_2"][0]
    for base_q, base_k, base_v in ((0, 1024, 1536), (512, 2048, 2560)):
        for p in range(4):
            job("ab", KD, 384, [(n * 128, 128, wab[:, b + p * 128:b + (p + 1) * 128])
                                for n, b in enumerate((base_q, base_k, base_v))])

    COLS = ((0, 384), (384, 768), (768, 1024))

    def tail_jobs(layer, w_out):
        for c0, c1 in COLS:
            job("out2", KD, c1 - c0, [(0, c1 - c0, w_out[:, c0:c1])])
        w1, w3, w2 = A["ffn_w1_2"][layer], A["ffn_w3_2"][layer], A["ffn_w2_2"][layer]
        for a, b in FPARTS:
            for j in range(a, b):
                job("up", KD, 256, [(0, 128, w1[:, j * P:(j + 1) * P]), (128, 128, w3[:, j * P:(j + 1) * P])], per=4)
            for n in range(2):
                job("down", b - a, 512, [(0, 512, w2[a * P:b * P, n * 512:(n + 1) * 512])])

    FPARTS = ((0, 6), (6, 12), (12, 17), (17, 22))
    tail_jobs(0, A["w_out_ab_2"][0])
    ada_jobs(1)
    wc = A["w_in_c_2"][0]
    for j in range(4):
        job("c", KD, 384, [(0, 256, wc[:, j * 256:(j + 1) * 256]), (256, 64, wc[:, D + j * 64:D + (j + 1) * 64]),
                           (320, 64, wc[:, D + 256 + j * 64:D + 256 + (j + 1) * 64])])
    tail_jobs(1, A["w_out_c_2"][0])

    pieces = [(n, i) for n, jb in enumerate(jobs) for i in range(len(jb[3]))]
    slab_state = {"loaded": 0, "split": 0, "used": 0}
    raw_free = [None] * 3
    slab_free = [None] * 2
    slab_ready = {}
    piece_arrived = {}

    def load_piece():
        m = slab_state["loaded"]
        if m >= len(pieces):
            return
        n, i = pieces[m]
        _, K, N, ps = jobs[n]
        k0, k1, segs = ps[i]
        view = raw[m % 3][:, 0:(k1 - k0) * N].rearrange("p (k n) -> p k n", n=N)
        for c, w, src in segs:
            tok = load(view[:, :, c:c + w], src, s_raw[m % 3], raw_free[m % 3])
        piece_arrived[m] = tok
        slab_state["loaded"] += 1

    def split_piece():
        m = slab_state["split"]
        n, i = pieces[m]
        _, K, N, ps = jobs[n]
        k0, k1, _ = ps[i]
        a, b = k0 * N, k1 * N
        src = raw[m % 3][:, 0:b - a]
        hi, lo = slab_hi[n % 2][:, a:b], slab_lo[n % 2][:, a:b]
        t_hi = act(lambda e: e.activation(hi, src, ACT.Copy), piece_arrived[m], slab_free[n % 2])
        t_lo = dve(lambda e: e.tensor_tensor(lo, src, hi.bitcast(F32), ALU.subtract), t_hi, piece_arrived[m])
        raw_free[m % 3] = [t_hi, t_lo]
        slab_ready[n] = [t_hi, t_lo]
        slab_state["split"] += 1
        load_piece()

    def pump():
        m = slab_state["split"]
        if m < len(pieces) and pieces[m][0] <= slab_state["used"] and jobs[pieces[m][0]][0] != "ada":
            split_piece()

    def next_slab(name):
        n = slab_state["used"]
        assert jobs[n][0] == name, (jobs[n][0], name)
        while slab_state["split"] < len(pieces) and pieces[slab_state["split"]][0] <= n:
            split_piece()
        slab_state["used"] += 1
        N = jobs[n][2]
        K = jobs[n][1]
        hi = slab_hi[n % 2][:, 0:K * N].rearrange("p (k n) -> p k n", n=N)
        lo = slab_lo[n % 2][:, 0:K * N].rearrange("p (k n) -> p k n", n=N)
        return n, hi, lo, slab_ready[n]

    def direct_piece(name):
        m = slab_state["split"]
        n, i = pieces[m]
        _, K, N, ps = jobs[n]
        assert jobs[n][0] == name and n == slab_state["used"], (jobs[n][0], n)
        slab_state["split"] += 1
        if i == len(ps) - 1:
            slab_state["used"] += 1

        def done(token):
            raw_free[m % 3] = token
            load_piece()
        return raw[m % 3][:, 0:K * N].rearrange("p (k n) -> p k n", n=N), piece_arrived[m], done

    def slab_done(n, token):
        slab_free[n % 2] = token

    def mm3(dst, lhs, rhs, first, last, *after):
        pe.wait(*after)
        (lh, ll), (rh, rl) = lhs, rhs
        pe(lambda e: e.matmul(dst, lh, rh, start=first, stop=False), signal=False)
        pe(lambda e: e.matmul(dst, lh, rl, start=False, stop=False), signal=False)
        return pe(lambda e: e.matmul(dst, ll, rh, start=False, stop=last), signal=last)

    def inv_rms(ss, width, *after):
        n = ss.shape[-1]
        half, y, a = stats(n), stats(n), stats(n)
        t = dve(lambda e: e.tensor_scalar(ss, ss, 1.0 / width, EPS, ALU.mult, ALU.add), *after)
        dve(lambda e: e.tensor_scalar(half, ss, -0.5, None, ALU.mult), t)
        t = dve(lambda e: e.tensor_scalar(a.bitcast(I32), ss.bitcast(I32), 1, None, ALU.logical_shift_right), t)
        t = dve(lambda e: e.tensor_scalar(y.bitcast(I32), a.bitcast(I32), -1.0, float(0x5F3759DF), ALU.mult, ALU.add), t)
        for step in range(3):
            t = dve(lambda e: e.tensor_tensor(a, y, y, ALU.mult), t)
            t = dve(lambda e: e.tensor_tensor(a, a, half, ALU.mult), t)
            t = dve(lambda e: e.scalar_tensor_tensor(ss if step == 2 else y, a, 1.5, y, ALU.add, ALU.mult), t)
        return t

    def normed_to_T(rows, ntiles, scratch, tmp, gain, shift, hi, lo, residue, *after):
        ss = stats(ntiles)
        for i in range(ntiles):
            t = act(lambda e, i=i: e.activation(scratch[:, i, :], rows[:, i, :], ACT.Square, accum_out=ss[:, i:i + 1]), *after)
        t = inv_rms(ss, D, t)
        for i in range(ntiles):
            t2 = dve(lambda e, i=i: e.tensor_scalar(scratch[:, i, :], rows[:, i, :], ss[:, i:i + 1], None, ALU.mult), t)
        w = ntiles * P
        for k in range(KD):
            bank, key = take_tr()
            for i in range(ntiles):
                tp = pe(lambda e, i=i: e.transpose(bank[:, i * P:(i + 1) * P], scratch[:, i, k * P:(k + 1) * P], ident[:, :]),
                        t2, free.get(key), free.get("const"), signal=(i == ntiles - 1))
            th = tmp[:, k % 2, 0:w]
            sh = shift(k) if shift else 0.0
            t3 = dve(lambda e, k=k, sh=sh, th=th, bank=bank: e.tensor_scalar(th, bank[:, 0:w], gain(k), sh, ALU.mult, ALU.add),
                     tp, free.get(("nt", k % 2)), free.get("cols"))
            free[key] = t3
            vi = (lambda ap: ap.rearrange("p (i r) -> p i r", r=RES)) if residue else (lambda ap: ap)
            vo = (lambda ap: ap.rearrange("p (r i) -> p i r", r=RES)) if residue else (lambda ap: ap)
            t4 = act(lambda e, k=k, th=th: e.activation(vo(hi(k)), vi(th), ACT.Copy), t3, *after)
            t5 = dve(lambda e, k=k, th=th: e.tensor_tensor(vo(lo(k)), vi(th), vo(hi(k).bitcast(F32)), ALU.subtract), t4)
            free[("nt", k % 2)] = [t4, t5]
        free["scratch"] = tp
        return t5

    def rows_to_T(y, ntiles, nchunks, hi, lo, residue, *after):
        w = ntiles * P
        vi = (lambda ap: ap.rearrange("p (r i) -> p r i", r=RES)) if residue else (lambda ap: ap)
        vo = (lambda ap: ap.rearrange("p (i r) -> p r i", r=RES)) if residue else (lambda ap: ap)
        for k in range(nchunks):
            bank, key = take_tr()
            for i in range(ntiles):
                tp = pe(lambda e, i=i, k=k, bank=bank: e.transpose(bank[:, i * P:(i + 1) * P], y[:, i, k * P:(k + 1) * P], ident[:, :]),
                        free.get(key), *after, signal=(i == ntiles - 1))
            t4 = act(lambda e, k=k, bank=bank: e.activation(vo(hi(k)), vi(bank[:, 0:w]), ACT.Copy), tp, *after)
            t5 = dve(lambda e, k=k, bank=bank: e.tensor_tensor(vo(lo(k)), vi(bank[:, 0:w]), vo(hi(k).bitcast(F32)), ALU.subtract), t4)
            free[key] = t5
        return t5

    def attend(q, segments, n, values, width, scale, probs, probsT, finish, sink=None, bias=None, after=()):
        for kT, c, w, mask in segments:
            last = mask is None
            t = pe(lambda e, kT=kT, c=c, w=w, last=last: e.matmul(score_ps[:, c:c + w], q, kT, start=True, stop=last),
                   free.get("scores"), *after)
            if mask is not None:
                t = pe(lambda e, c=c, w=w, mask=mask: e.matmul(score_ps[:, c:c + w], identb[:, :], mask, start=False, stop=True),
                       free.get("masks"))
        st = stats(4)
        mx, nm, den, rden = (st[:, i:i + 1] for i in range(4))
        if bias is None:
            t = dve(lambda e: e.reduce_max(mx, score_ps[:, 0:n], AX.X), t)
            if sink is None:
                t = dve(lambda e: e.tensor_scalar(nm, mx, -scale, None, ALU.mult), t)
            else:
                t = dve(lambda e: e.scalar_tensor_tensor(mx, mx, scale, sink, ALU.mult, ALU.max), t)
                t = dve(lambda e: e.tensor_scalar(nm, mx, -1.0, None, ALU.mult), t)
            t = act(lambda e: e.activation(probs[:, 0:n], score_ps[:, 0:n], ACT.Exp, bias=nm, scale=scale, accum_out=den),
                    t, free.get("probs"))
            free["scores"] = t
        else:
            btab, btok = bias
            t1 = dve(lambda e: e.scalar_tensor_tensor(probs[:, 0:512], score_ps[:, 0:512], scale, btab, ALU.mult, ALU.add),
                     t, btok, free.get("probs"))
            t1 = dve(lambda e: e.tensor_scalar(probs[:, 512:n], score_ps[:, 512:n], scale, None, ALU.mult), t)
            free["scores"] = t1
            t = dve(lambda e: e.reduce_max(mx, probs[:, 0:n], AX.X), t1)
            t = dve(lambda e: e.tensor_scalar(nm, mx, -1.0, None, ALU.mult), t)
            t = act(lambda e: e.activation(probs[:, 0:n], probs[:, 0:n], ACT.Exp, bias=nm, accum_out=den), t)
        tprob = t
        if sink is not None:
            es = stats(1)
            t = act(lambda e: e.activation(es, sink, ACT.Exp, bias=nm), t)
            t = dve(lambda e: e.tensor_tensor(den, den, es, ALU.add), t)
        trden = dve(lambda e: e.reciprocal(rden, den), t)
        yield
        t = yield from transposed(probs, n, probsT, tprob)
        t = weigh(probsT, n, values, width, t)
        free["outp"] = finish(out_ps[:, 0:width], rden, [t, trden])
        yield

    def transposed(probs, n, probsT, ready):
        toks = []
        for b0 in range(0, n, 512):
            b1 = min(n, b0 + 512)
            bank, key = take_tr()
            for c in range(b0, b1, P):
                tp = pe(lambda e, c=c, bank=bank, b0=b0: e.transpose(bank[:, c - b0:c - b0 + P], probs[:, c:c + P], ident[:, :]),
                        ready, free.get(key), signal=(c + P >= b1))
            if b0 == 0:
                t = dve(lambda e, bank=bank, b0=b0, b1=b1: e.tensor_copy(probsT[:, b0:b1], bank[:, 0:b1 - b0]), tp, free.get("probsT"))
            else:
                t = act(lambda e, bank=bank, b0=b0, b1=b1: e.activation(probsT[:, b0:b1], bank[:, 0:b1 - b0], ACT.Copy), tp, free.get("probsT"))
            free[key] = t
            toks.append(t)
        free["probs"] = tp
        yield
        return toks

    def weigh(probsT, n, values, width, ready):
        for j in range(n // P):
            t = pe(lambda e, j=j: e.matmul(out_ps[:, 0:width], probsT[:, j * P:(j + 1) * P], values[j], start=(j == 0), stop=(j == n // P - 1)),
                   ready, free.get("outp"), free.get("values"), signal=(j == n // P - 1))
        free["probsT"] = t
        return t

    def scaled_into(dst):
        def finish(o, rden, t):
            return act(lambda e: e.activation(dst, o, ACT.Copy, scale=rden), t)
        return finish

    def to_T(raw_ap, tiles, bank_w, dst, scale_col, *after):
        for b0 in range(0, tiles, 4):
            b1 = min(tiles, b0 + 4)
            bank, key = take_tr()
            for i in range(b0, b1):
                tp = pe(lambda e, i=i, bank=bank, b0=b0: e.transpose(bank[:, (i - b0) * P:(i - b0 + 1) * P], raw_ap(i), ident[:, :]),
                        free.get(key), *after, signal=(i == b1 - 1))
            src = bank[:, 0:(b1 - b0) * P]
            d = dst[:, b0 * P:b1 * P]
            if scale_col is None:
                t = act(lambda e, d=d, src=src: e.activation(d, src, ACT.Copy), tp, *after)
            else:
                t = dve(lambda e, d=d, src=src: e.tensor_scalar(d, src, scale_col, None, ALU.mult), tp, *after)
            free[key] = t
        return t

    def head_norms(view, nheads, width, sq, *after):
        ss = stats(nheads)
        t = act(lambda e: e.activation(sq, view, ACT.Square), *after)
        t = dve(lambda e: e.tensor_reduce(ss, sq, AX.X, ALU.add), t)
        t = inv_rms(ss, width, t)
        return dve(lambda e: e.tensor_tensor(view, view, ss.unsqueeze(2).to_broadcast([P, nheads, width]), ALU.mult), t)

    for _ in range(3):
        load_piece()
    load(ident[:, :], A["ident"], s_const)
    load(gcol[:, 0:6, :], A["gain_cols"].rearrange("p (n k) -> p n k", k=KD), s_const)
    for n in range(2):
        load(gmem[:, n, :], A["mem_q_gain"][n:n + 1, :].to_broadcast([P, HD]), s_const)
        load(gmem[:, 2 + n, :], A["mem_k_gain"][n:n + 1, :].to_broadcast([P, HD]), s_const)
    t_x = load(x[:, :, :], A["x"][0].rearrange("(i p) d -> p i d", p=P), s_x)
    t_const = s_const.token()
    free["cols"] = t_const
    t = dve(lambda e: e.memset(ones[:, :], 1.0))
    free["const"] = [t_const, dve(lambda e: e.tensor_copy(identb[:, :], ident[:, :]), t_const)]
    all_done = lambda: [pe.last(), act.last(), dve.last(), pool.last()]

    def fence():
        toks = all_done()
        for e in (pe, act, dve, pool, sp):
            e.wait(*toks)

    x_hi, x_lo = (lambda k: hx_hi[:, k, :]), (lambda k: hx_lo[:, k, :])
    finished = {"v": False}

    def dump(view):
        fence()
        load(out[0].rearrange("(i p) d -> p i d", p=P), view, s_out)
        sp.wait(s_out.token())
        finished["v"] = True

    def first_block_layer(layer):
        st = contextlib.ExitStack()
        loc = lambda n, shape, dt=F32: sb_in(st, f"l{layer}_{n}", shape, dt)
        y = loc("y", [P, NT, MIX])
        with contextlib.ExitStack() as s0:
            tmp = sb_in(s0, f"l{layer}_tmp", [P, 2, 512])
            scratch = y[:, :, 0:D]
            t = normed_to_T(x, NT, scratch, tmp, lambda k: gcol[:, layer, k:k + 1], None, x_hi, x_lo, layer == 0, t_x)
            fence()
        if layer == 0:
            dilated_heads(y)
        else:
            gated_heads(y)
        fence()
        s1 = contextlib.ExitStack()
        memx = sb_in(s1, f"m{layer}_memx", [P, NC, D])
        mtmp = sb_in(s1, f"m{layer}_tmp", [P, 2, 512])
        kmT = sb_in(s1, f"m{layer}_kmT", [P, MH, CTX])
        vm = sb_in(s1, f"m{layer}_vm", [P, NC, MH, HD])
        kraw = sb_in(s1, f"m{layer}_kraw", [P, NC, HD])
        sq = sb_in(s1, f"m{layer}_sq", [P, NT, 2, HD])
        s2 = contextlib.ExitStack()
        m_hi = sb_in(s2, f"m{layer}_hi", [P, KD, CTX], F32R)
        m_lo = sb_in(s2, f"m{layer}_lo", [P, KD, CTX], F32R)
        t_mem = load(memx[:, :, :], A["mem"][0].rearrange("(i p) d -> p i d", p=P), s_misc[0])
        mscr = sb_in(s2, f"m{layer}_scr", [P, NC, D])
        th = normed_to_T(memx, NC, mscr, mtmp, lambda k: gcol[:, 2 + layer, k:k + 1], None,
                         lambda k: m_hi[:, k, :], lambda k: m_lo[:, k, :], False, t_mem)
        for m in range(MH):
            n, wh, wl, ready = next_slab("mkv")
            for i in range(NC):
                ps, key = take_proj()
                for k in range(KD):
                    tk = (slice(None), k, slice(i * P, (i + 1) * P))
                    t = mm3(ps[:, 0:256], (m_hi[tk], m_lo[tk]), (wh[:, k, :], wl[:, k, :]), k == 0, k == KD - 1, ready, th, free.get(key))
                pump()
                t1 = act(lambda e, i=i, ps=ps: e.activation(kraw[:, i, :], ps[:, 0:128], ACT.Copy), t, free.get("kraw"))
                t2 = act(lambda e, i=i, m=m, ps=ps: e.activation(vm[:, i, m, :], ps[:, 128:256], ACT.Copy), t)
                free[key] = t2
            slab_done(n, t)
            t = head_norms(kraw[:, :, :], NC, HD, sq[:, 0:NC, 0, :], t2)
            t = dve(lambda e: e.tensor_tensor(kraw[:, :, :], kraw[:, :, :],
                                              gmem[:, 2 + layer, :].unsqueeze(1).to_broadcast([P, NC, HD]), ALU.mult), t)
            free["kraw"] = t_k = to_T(lambda i: kraw[:, i, :], NC, 0, kmT[:, m, :], None, t)
        fence()
        s2.close()
        qraw = sb_in(s1, f"m{layer}_qraw", [P, NT, 2, HD])
        qT = sb_in(s1, f"m{layer}_qT", [P, 2, S])
        probs = sb_in(s1, f"m{layer}_probs", [P, CTX])
        probsT = sb_in(s1, f"m{layer}_probsT", [P, CTX])
        for half in range(2):
            n, wh, wl, ready = next_slab("mq")
            for i in range(NT):
                ps, key = take_proj()
                for k in range(KD):
                    tk = (slice(None), k, slice(i * P, (i + 1) * P))
                    t = mm3(ps[:, 0:256], (hx_hi[tk], hx_lo[tk]), (wh[:, k, :], wl[:, k, :]), k == 0, k == KD - 1, ready, free.get(key))
                pump()
                t1 = act(lambda e, i=i, ps=ps: e.activation(qraw[:, i, :, :].rearrange("p a d -> p (a d)"), ps[:, 0:256], ACT.Copy), t, free.get("qraw"))
                free[key] = t1
            slab_done(n, t)
            q8 = qraw[:, :, :, :].rearrange("p i a d -> p (i a) d")
            t = head_norms(q8, 2 * NT, HD, sq[:, :, :, :].rearrange("p i a d -> p (i a) d"), t1)
            t = dve(lambda e: e.tensor_tensor(q8, q8, gmem[:, layer, :].unsqueeze(1).to_broadcast([P, 2 * NT, HD]), ALU.mult), t)
            for a in range(2):
                tq = to_T(lambda i, a=a: qraw[:, i, a, :], NT, 0, qT[:, a, :], None, t, free.get("qT"))
            free["qraw"] = tq
            for a in range(2):
                m = half * 2 + a
                for i in range(NT):
                    for _ in attend(qT[:, a, i * P:(i + 1) * P], [(kmT[:, m, :], 0, CTX, None)], CTX,
                                    [vm[:, j, m, :] for j in range(NC)], HD, HD ** -0.5, probs, probsT,
                                    scaled_into(y[:, i, AH * HD + m * HD:AH * HD + (m + 1) * HD]), after=[tq, t_k]):
                        pass
            free["qT"] = pe.last()
        sg = sb_in(s1, f"m{layer}_sg", [P, 2, 384])
        for c in range(MIX // 384):
            n, wh, wl, ready = next_slab("gate")
            for i in range(NT):
                ps, key = take_proj()
                for k in range(KD):
                    tk = (slice(None), k, slice(i * P, (i + 1) * P))
                    t = mm3(ps[:, 0:384], (hx_hi[tk], hx_lo[tk]), (wh[:, k, :], wl[:, k, :]), k == 0, k == KD - 1, ready, free.get(key))
                pump()
                g = sg[:, i % 2, :]
                t1 = act(lambda e, g=g, ps=ps: e.activation(g, ps[:, 0:384], ACT.Silu), t, free.get(("sg", i % 2)))
                free[key] = t1
                yv = y[:, i, c * 384:(c + 1) * 384]
                free[("sg", i % 2)] = dve(lambda e, g=g, yv=yv: e.tensor_tensor(yv, yv, g, ALU.mult), t1, act.last())
            slab_done(n, t)
        fence()
        s1.close()
        s3 = contextlib.ExitStack()
        y_hi = sb_in(s3, f"o{layer}_hi", [P, 4, S], F32R)
        y_lo = sb_in(s3, f"o{layer}_lo", [P, 4, S], F32R)
        yh = lambda k: hx_hi[:, k, :] if k < KD else y_hi[:, k - KD, :]
        yl = lambda k: hx_lo[:, k, :] if k < KD else y_lo[:, k - KD, :]
        th = rows_to_T(y, NT, MIX // P, yh, yl, layer == 0)
        for c in range(4):
            n, wh, wl, ready = next_slab("out")
            for i in range(NT):
                ps, key = take_proj()
                for k in range(MIX // P):
                    pick = lambda ap: ap[:, i * P:(i + 1) * P]
                    t = mm3(ps[:, 0:256], (pick(yh(k)), pick(yl(k))), (wh[:, k, :], wl[:, k, :]), k == 0, k == MIX // P - 1, ready, th, free.get(key))
                pump()
                xv = x[:, i, c * 256:(c + 1) * 256]
                free[key] = dve(lambda e, xv=xv, ps=ps: e.tensor_tensor(xv, xv, ps[:, 0:256], ALU.add), t)
            slab_done(n, t)
        fence()
        s3.close()
        st.close()

    def dilated_heads(y):
        st = contextlib.ExitStack()
        loc = lambda n, shape, dt=F32: sb_in(st, f"a_{n}", shape, dt)
        masks = loc("masks", [P, RES, 768], BF16)
        qk_raw = loc("qk_raw", [P, NT, 2, HD])
        qT = [loc(f"qT{i}", [P, NG, S]) for i in range(2)]
        kT = [loc(f"kT{i}", [P, NG, S]) for i in range(2)]
        vv = [loc(f"v{i}", [P, NG, NT, HD]) for i in range(2)]
        probs = loc("probs", [P, 768])
        probsT = loc("probsT", [P, 768])
        sq = loc("sq", [P, NT, 2, HD])
        rope = loc("rope", [P, 4, NG, NT, 2, HALF])
        rt = loc("rt", [P, 4, NT, 2, HALF])
        gT = loc("gT", [P, 2, NG])
        for r in range(RES):
            tl = load(probs[:, :], A["mask_a"][:, r * 768:(r + 1) * 768], s_misc[1], dve.last() if r else None)
            t_mask = dve(lambda e, r=r: e.tensor_copy(masks[:, r, :], probs[:, :]), tl)
        free["masks"] = [t_mask, free["const"]]
        load(gT[:, :, :], A["gain_a_cols"].rearrange("p (a g) -> p a g", g=NG), s_misc[2])
        with contextlib.ExitStack() as s0:
            pi = sb_in(s0, "r_pi", [P, NT], I32)
            pf = sb_in(s0, "r_pf", [P, NT])
            inv = sb_in(s0, "r_inv", [P, HALF])
            ang = sb_in(s0, "r_ang", [P, 2, NT, HALF])
            kk = rt[:, 0, :, 0, :]
            ga = probsT[:, 0:2 * NG * ROT].rearrange("p (a g c) -> p a g c", a=2, g=NG)
            load(pi[:, :], A["positions"][0].rearrange("(i r) -> i r", r=RES), s_misc[2])
            load(inv[:, :], A["inv_freq"], s_misc[2])
            load(ga[:, 0, :, :], A["q_gain_a"][:, :, 0:ROT].to_broadcast([P, NG, ROT]), s_misc[2])
            tl = load(ga[:, 1, :, :], A["k_gain_a"][:, :, 0:ROT].to_broadcast([P, NG, ROT]), s_misc[2])
            t = dve(lambda e: e.tensor_copy(pf[:, :], pi[:, :]), tl)
            a1, a0 = ang[:, 1], ang[:, 0]
            t = dve(lambda e: e.tensor_tensor(a1, pf[:, :].unsqueeze(2).to_broadcast([P, NT, HALF]),
                                              inv[:, :].unsqueeze(1).to_broadcast([P, NT, HALF]), ALU.mult), t)
            magic = 12582912.0
            t = dve(lambda e: e.tensor_scalar(kk, a1, 1.0 / (2 * math.pi), magic, ALU.mult, ALU.add), t)
            t = dve(lambda e: e.tensor_scalar(kk, kk, magic, None, ALU.subtract), t)
            c1 = 6.28125
            c2 = math.floor((2 * math.pi - c1) * 2 ** 20) / 2 ** 20
            c3 = 2 * math.pi - c1 - c2
            for cpart in (c1, c2, c3):
                t = dve(lambda e, cpart=cpart: e.scalar_tensor_tensor(a1, kk, -cpart, a1, ALU.mult, ALU.add), t)
            t = dve(lambda e: e.tensor_scalar(a0, a1, math.pi / 2, None, ALU.add), t)
            t = dve(lambda e: e.tensor_scalar(kk, a0, math.pi, -2 * math.pi, ALU.is_gt, ALU.mult), t)
            t = dve(lambda e: e.tensor_tensor(a0, a0, kk, ALU.add), t)
            t = dve(lambda e: e.tensor_scalar(ang[:, :, :, :], ang[:, :, :, :], 3.1415925, -3.1415925, ALU.min, ALU.max), t)
            t = act(lambda e: e.activation(ang[:, :, :, :], ang[:, :, :, :], ACT.Sin), t)
            for g in range(NG):
                for n, (which, part) in enumerate(((0, 0), (1, 1), (0, 1), (1, 0))):
                    for b in range(2):
                        t2 = dve(lambda e, g=g, n=n, which=which, part=part, b=b: e.tensor_tensor(
                            rope[:, n, g, :, b, :], ang[:, which],
                            ga[:, b, g, part * HALF:(part + 1) * HALF].unsqueeze(1).to_broadcast([P, NT, HALF]), ALU.mult), t)
            t_rope = t2
            fence()

        def project(h):
            b = h % 2
            for g in range(NG):
                n, wh, wl, ready = next_slab("a")
                for i in range(NT):
                    ps, key = take_proj()
                    for k in range(KD):
                        tk = (slice(None), k, slice(i * P, (i + 1) * P))
                        t = mm3(ps[:, 0:384], (hx_hi[tk], hx_lo[tk]), (wh[:, k, :], wl[:, k, :]), k == 0, k == KD - 1, ready, free.get(key))
                    t1 = act(lambda e, i=i, ps=ps: e.activation(qk_raw[:, i, :, :].rearrange("p a d -> p (a d)"), ps[:, 0:256], ACT.Copy), t, free.get("qk_raw"))
                    free[key] = act(lambda e, i=i, ps=ps, g=g: e.activation(vv[b][:, g, i, :], ps[:, 256:384], ACT.Copy), t, free.get(("head", b)))
                    pump()
                    if i == NT - 1:
                        slab_done(n, t)
                        rope_and_turn(h, g, t1)
                    yield

        def rope_and_turn(h, g, ready):
            b = h % 2
            v8 = qk_raw[:, :, :, :].rearrange("p i a d -> p (i a) d")
            t = head_norms(v8, 2 * NT, HD, sq[:, :, :, :].rearrange("p i a d -> p (i a) d"), ready, free.get("sq"))
            x1, x2 = v8[:, :, 0:HALF], v8[:, :, HALF:ROT]
            tab = lambda n: rope[:, n, g, :, :, :].rearrange("p i a c -> p (i a) c")
            r_ = lambda n: rt[:, n, :, :, :].rearrange("p i a c -> p (i a) c")
            ta = dve(lambda e: e.tensor_tensor(r_(0), x1, tab(0), ALU.mult), t)
            tb = dve(lambda e: e.tensor_tensor(r_(1), x2, tab(1), ALU.mult), t)
            tc = dve(lambda e: e.tensor_tensor(r_(2), x2, tab(2), ALU.mult), t)
            td = dve(lambda e: e.tensor_tensor(r_(3), x1, tab(3), ALU.mult), t)
            te = dve(lambda e: e.tensor_tensor(x1, r_(0), r_(1), ALU.subtract), td)
            tf = dve(lambda e: e.tensor_tensor(x2, r_(2), r_(3), ALU.add), td)
            to_T(lambda i: qk_raw[:, i, 0, :], NT, 0, qT[b][:, g, :], gT[:, 0, g:g + 1], tf, free.get(("head", b)))
            free["qk_raw"] = to_T(lambda i: qk_raw[:, i, 1, :], NT, 0, kT[b][:, g, :], gT[:, 1, g:g + 1], tf)
            free[("qk", b, g)] = [dve.last(), act.last()]

        def attention(h):
            b = h % 2
            for r in range(RES):
                q = [qT[b][:, g, r * P:(r + 1) * P] for g in range(NG)]
                first = [(q[0], kT[b][:, 0, :], 0, 512)] + [(q[g], kT[b][:, g, r * P:(r + 1) * P], 384 + g * P, P) for g in (1, 2)]
                for qq, kk_, c, w in first:
                    pe(lambda e, qq=qq, kk_=kk_, c=c, w=w: e.matmul(score_ps[:, c:c + w], qq, kk_, start=True, stop=False),
                       free.get("scores"), [free[("qk", b, g)] for g in range(NG)], signal=False)
                    t = pe(lambda e, c=c, w=w, r=r: e.matmul(score_ps[:, c:c + w], identb[:, :], masks[:, r, c:c + w], start=False, stop=True), free["masks"])
                st4 = stats(4)
                mx, nm, den, rden = (st4[:, i:i + 1] for i in range(4))
                t = dve(lambda e: e.reduce_max(mx, score_ps[:, 0:768], AX.X), t)
                t = dve(lambda e: e.tensor_scalar(nm, mx, -(HD ** -0.5), None, ALU.mult), t)
                tprob = act(lambda e: e.activation(probs[:, :], score_ps[:, 0:768], ACT.Exp, bias=nm, scale=HD ** -0.5, accum_out=den), t, free.get("probs"))
                free["scores"] = tprob
                tr_ = dve(lambda e: e.reciprocal(rden, den), tprob)
                yield
                tt = yield from transposed(probs, 768, probsT, tprob)
                values = [vv[b][:, 0, j, :] for j in range(NT)] + [vv[b][:, g, r, :] for g in (1, 2)]
                t = weigh(probsT, 768, values, HD, tt)
                dst = y[:, r, h * HD:(h + 1) * HD]
                free["outp"] = act(lambda e, dst=dst: e.activation(dst, out_ps[:, 0:HD], ACT.Copy, scale=rden), t, tr_)
                yield
            free[("head", b)] = pe.last()

        for _ in project(0):
            pass
        for h in range(AH):
            weave(project(h + 1) if h + 1 < AH else iter(()), attention(h))
        fence()
        st.close()

    def gated_heads(y):
        st = contextlib.ExitStack()
        loc = lambda n, shape, dt=F32: sb_in(st, f"b_{n}", shape, dt)
        carry = loc("carry", [P, S])
        lmask = loc("lmask", [P, 8, P])
        og = loc("og", [P, HD])
        lb = loc("lb", [P, 4, AH])
        qT = [loc(f"qT{i}", [P, S]) for i in range(2)]
        kT = [loc(f"kT{i}", [P, S]) for i in range(2)]
        G = [loc(f"G{i}", [P, S]) for i in range(2)]
        vT = loc("vT", [P, S])
        vN = [loc(f"vN{i}", [P, NT, HD]) for i in range(2)]
        w1 = loc("w1", [P, S])
        w2 = loc("w2", [P, S])
        E = loc("E", [P, S])
        qd = [loc(f"qd{i}", [P, S]) for i in range(2)]
        kd = [loc(f"kd{i}", [P, S]) for i in range(2)]
        attn = loc("attn", [P, NT, P])
        kdN = loc("kdN", [P, NT - 1, P])
        state = loc("state", [P, NT - 1, HD])
        lv = w1
        tl = load(carry[:, :], A["carry"], s_misc[3])
        load(lmask[:, :, :], A["level_mask"].rearrange("p (l t) -> p l t", l=8), s_misc[3])
        load(og[:, :], A["o_gain_b"].to_broadcast([P, HD]), s_misc[3])
        tl = load(lb[:, 0:2, :], A["lb_cols"].rearrange("p (n k) -> p n k", k=AH), s_misc[3])
        l0, l1, l2, l3 = (lb[:, i, :] for i in range(4))
        t = dve(lambda e: e.tensor_tensor(l2, l0, l1, ALU.max), tl)
        t = dve(lambda e: e.tensor_tensor(l0, l0, l2, ALU.subtract), t)
        t = dve(lambda e: e.tensor_tensor(l1, l1, l2, ALU.subtract), t)
        t = act(lambda e: e.activation(lb[:, 0:2, :], lb[:, 0:2, :], ACT.Exp), t)
        t = dve(lambda e: e.tensor_tensor(l2, l0, l1, ALU.add), t)
        t = dve(lambda e: e.reciprocal(l2, l2), t)
        t = dve(lambda e: e.tensor_tensor(l1, l1, l2, ALU.mult), t)
        t_lb = dve(lambda e: e.tensor_scalar(l3, l1, -1.0, 1.0, ALU.mult, ALU.add), t)

        def project(h):
            b = h % 2
            n, wh, wl, ready = next_slab("b")
            lbc, omc = lb[:, 1, h:h + 1], lb[:, 3, h:h + 1]
            for part in range(3):
                ps, key = take_proj()
                for k in range(KD):
                    cs = slice(part * P, (part + 1) * P)
                    t = mm3(ps[:, :], (wh[:, k, cs], wl[:, k, cs]), (hx_hi[:, k, :], hx_lo[:, k, :]), k == 0, k == KD - 1, ready, free.get(key))
                pump()
                hb = free.get(("head", b))
                if part == 0:
                    free[key] = act(lambda e, ps=ps: e.activation(qT[b][:, :], ps[:, :], ACT.Copy), t, hb)
                elif part == 1:
                    ee, rr = kT[b][:, :], G[b][:, :]
                    t1 = dve(lambda e, ps=ps: e.tensor_scalar(ee, ps[:, :], -80.0, None, ALU.max), t, hb)
                    free[key] = t1
                    t1 = act(lambda e: e.activation(ee, ee, ACT.Exp, scale=-1.0), t1)
                    t1 = dve(lambda e: e.tensor_scalar(rr, ee, 1.0, None, ALU.add), t1)
                    t1 = dve(lambda e: e.reciprocal(rr, rr), t1)
                    t2 = dve(lambda e: e.scalar_tensor_tensor(ee, ee, omc, rr, ALU.mult, ALU.mult), t1, t_lb)
                    t1 = dve(lambda e: e.tensor_scalar(rr, rr, omc, lbc, ALU.mult, ALU.add), t2)
                    t1 = act(lambda e: e.activation(rr, rr, ACT.Ln), t1)
                    t1 = dve(lambda e: e.tensor_tensor_scan(rr, carry[:, :], rr, 0.0, ALU.mult, ALU.add), t1)
                    free[("kg", b)] = t1
                else:
                    t1 = act(lambda e, ps=ps: e.activation(vT[:, :], ps[:, :], ACT.Copy), t, free.get("vT"))
                    free[key] = t1
                    tv = to_T(lambda i: vT[:, i * P:(i + 1) * P], NT, 0, vN[b][:, :, :].rearrange("p i d -> p (i d)"), None, t1, hb)
                    free["vT"] = tv
                    free[("v", b)] = tv
                    slab_done(n, t)
                yield

        def scan(h):
            b = h % 2
            kg = [free[("kg", b)], free[("v", b)], act.last()]
            chunked = lambda ap: ap.rearrange("p (c t) -> p c t", t=CHUNK)
            for n in range(8):
                j = n % 2
                if n < 7:
                    L = LEVELS[n]
                    pairs = lambda ap, L=L: ap.rearrange("p (m two l) -> p m two l", two=2, l=L)
                    g4, e4 = pairs(G[b][:, :]), pairs(E[:, :])
                    ref = g4[:, :, 0, L - 1:L].to_broadcast([P, S // (2 * L), L])
                    t1 = dve(lambda e, g4=g4, e4=e4, ref=ref: e.tensor_tensor(e4[:, :, 0, :], ref, g4[:, :, 0, :], ALU.subtract), kg, free.get("E"))
                    t1 = dve(lambda e, g4=g4, e4=e4, ref=ref: e.tensor_tensor(e4[:, :, 1, :], g4[:, :, 1, :], ref, ALU.subtract), kg)
                    t1 = act(lambda e: e.activation(E[:, :], E[:, :], ACT.Exp), t1)
                    tq = dve(lambda e, j=j: e.tensor_tensor(qd[j][:, :], qT[b][:, :], E[:, :], ALU.mult), t1, free.get(("qd", j)))
                    tk = pool(lambda e, j=j: e.tensor_tensor(kd[j][:, :], kT[b][:, :], E[:, :], ALU.mult), t1, kg, free.get(("qd", j)))
                    free["E"] = [tq, tk]
                    q_, k_ = qd[j], kd[j]
                else:
                    tq, tk, q_, k_ = kg, None, qT[b], kT[b]
                bank, bkey = (score_ps[:, j * 512:(j + 1) * 512], ("scores", j))
                for c in range(NT):
                    cs = slice(c * P, (c + 1) * P)
                    t = pe(lambda e, cs=cs, bank=bank, q_=q_, k_=k_: e.matmul(bank[:, cs], k_[:, cs], q_[:, cs], start=True, stop=True),
                           tq, tk, free.get(bkey), free.get("scores"), signal=(c == NT - 1))
                free[("qd", j)] = t
                mk = lmask[:, n, :].unsqueeze(1).to_broadcast([P, NT, P])
                src = bank.rearrange("p (c t) -> p c t", t=P)
                if n == 0:
                    ta = dve(lambda e, src=src, mk=mk: e.tensor_tensor(attn[:, :, :], src, mk, ALU.mult), t, free.get("attn"))
                    free[bkey] = ta
                else:
                    lvv = w1[:, :].rearrange("p (c t) -> p c t", t=P)
                    ta = dve(lambda e, src=src, mk=mk, lvv=lvv: e.tensor_tensor(lvv, src, mk, ALU.mult), t, free.get("w1"))
                    free[bkey] = ta
                    ta = pool(lambda e, lvv=lvv: e.tensor_tensor(attn[:, :, :], attn[:, :, :], lvv, ALU.add), ta)
                    free["w1"] = ta
                yield
            t1 = act(lambda e: e.activation(E[:, :], G[b][:, :], ACT.Exp), kg, free.get("E"))
            tq = dve(lambda e: e.tensor_tensor(qd[0][:, :], qT[b][:, :], E[:, :], ALU.mult), t1, free.get(("qd", 0)))
            glast = stats(NT)
            t2 = dve(lambda e: e.tensor_copy(glast, chunked(E[:, :])[:, :, P - 1]), t1)
            t3 = dve(lambda e: e.tensor_tensor(chunked(w2[:, :]), chunked(G[b][:, :])[:, :, P - 1:P].to_broadcast([P, NT, P]),
                                               chunked(G[b][:, :]), ALU.subtract), kg, free.get("w2"))
            t3 = act(lambda e: e.activation(w2[:, :], w2[:, :], ACT.Exp), t3)
            t3 = dve(lambda e: e.tensor_tensor(kd[0][:, :], kT[b][:, :], w2[:, :], ALU.mult), t3, free.get(("qd", 0)))
            free["w2"] = t3
            free["E"] = [tq, t2]
            tkd = to_T(lambda i: kd[0][:, i * P:(i + 1) * P], NT - 1, 0, kdN[:, :, :].rearrange("p i d -> p (i d)"), None, t3, free.get("kdN"))
            yield
            tstate = None
            for c in range(NT):
                cs = slice(c * P, (c + 1) * P)
                t = pe(lambda e, c=c: e.matmul(out_ps[:, 0:HD], attn[:, c, :], vN[b][:, c, :], start=True, stop=(c == 0)), ta, kg, free.get("outp"))
                if c:
                    t = pe(lambda e, c=c, cs=cs: e.matmul(out_ps[:, 0:HD], qd[0][:, cs], state[:, c - 1, :], start=False, stop=True), tq, tstate)
                free["outp"] = act(lambda e, c=c: e.activation(y[:, c, h * HD:(h + 1) * HD], out_ps[:, 0:HD], ACT.Copy), t)
                if c < NT - 1:
                    bank, key = take_tr()
                    ts = pe(lambda e, c=c, bank=bank: e.matmul(bank[:, 0:HD], kdN[:, c, :], vN[b][:, c, :], start=True, stop=True), tkd, free.get(key))
                    if c == 0:
                        tstate = dve(lambda e, bank=bank: e.tensor_copy(state[:, 0, :], bank[:, 0:HD]), ts, free.get("state"))
                    else:
                        tstate = dve(lambda e, c=c, bank=bank: e.scalar_tensor_tensor(state[:, c, :], state[:, c - 1, :], glast[:, c:c + 1], bank[:, 0:HD],
                                                                                     ALU.mult, ALU.add), ts, tstate, t2)
                    free[key] = tstate
                yield
            free["attn"] = free["state"] = free["kdN"] = free[("head", b)] = t
            free[("qd", 0)] = t
            yv = y[:, :, h * HD:(h + 1) * HD]
            t = head_norms(yv, NT, HD, w2[:, :].rearrange("p (i d) -> p i d", d=HD), free["outp"], free["w2"])
            free["w2"] = t
            dve(lambda e: e.tensor_tensor(yv, yv, og[:, :].unsqueeze(1).to_broadcast([P, NT, HD]), ALU.mult), t)
            yield

        for _ in project(0):
            pass
        for h in range(AH):
            weave(project(h + 1) if h + 1 < AH else iter(()), scan(h), 5)
        fence()
        st.close()

    def second_block():
        ctxs = contextlib.ExitStack()
        keep = lambda n, shape, dt=F32: sb_in(ctxs, f"s_{n}", shape, dt)
        cx = keep("ctx", [P, NC, D])
        hc_hi = keep("hc_hi", [P, KD, CTX], F32R)
        hc_lo = keep("hc_lo", [P, KD, CTX], F32R)
        cs = keep("cs", [P, 2, KD])
        csT = keep("csT", [P, KD, 2])
        adab = keep("adab", [P, 2, 6 * KD])
        g2 = keep("g2", [P, 2, 2, KD])
        mod = keep("mod", [P, 6, KD, 2])
        amp = keep("amp", [P, 2, KD, 2])
        cos2 = keep("cos2", [P, NT, HD2])
        sin2 = keep("sin2", [P, NT, HD2])
        c_hi, c_lo = (lambda k: hc_hi[:, k, :]), (lambda k: hc_lo[:, k, :])
        load(cs[:, :, :], A["c_cols"].rearrange("p (a k) -> p a k", k=KD), s_misc[4])
        load(adab[:, :, :], A["ada_b_cols"].rearrange("p (l n) -> p l n", l=2), s_misc[4])
        load(g2[:, :, :, :], A["gain_cols_2"].rearrange("p (l a k) -> p l a k", l=2, a=2), s_misc[4])
        load(cos2[:, :, :], A["cos2"].rearrange("(i p) c -> p i c", p=P), s_misc[4])
        load(sin2[:, :, :], A["sin2"].rearrange("(i p) c -> p i c", p=P), s_misc[4])
        t_in = load(cx[:, :, :], A["ctx_2"][0].rearrange("(i p) d -> p i d", p=P), s_misc[4])
        t = act(lambda e: e.activation(cs[:, :, :], cs[:, :, :], ACT.Silu), t_in)
        t_cs = dve(lambda e: e.tensor_copy(csT[:, :, :], cs[:, :, :].rearrange("p a k -> p k a")), t)

        x_tiles = [((lambda k, i=i: hx_hi[:, k, i * P:(i + 1) * P]), (lambda k, i=i: hx_lo[:, k, i * P:(i + 1) * P])) for i in range(NT)]
        c_tiles = [((lambda k, i=i: hc_hi[:, k, i * P:(i + 1) * P]), (lambda k, i=i: hc_lo[:, k, i * P:(i + 1) * P])) for i in range(NC)]

        def modulations(layer):
            bank, key = take_proj()
            for n in range(32):
                piece, arrived, done = direct_piece("ada")
                for f in range(3):
                    c0 = n * 192 + f * 64
                    chunk, part = c0 // P, (c0 % P)
                    for k in range(KD):
                        last = k == KD - 1
                        t = pe(lambda e: e.matmul(bank[part:part + 64, 2 * chunk:2 * chunk + 2], piece[:, k, f * 64:(f + 1) * 64], csT[:, k, :],
                                                  start=(k == 0), stop=last), arrived, t_cs, free.get(key), signal=last)
                done(t)
            m96 = mod[:, :, :, :].rearrange("p a k c -> p (a k) c")
            t = dve(lambda e: e.tensor_tensor(m96, bank[:, 0:96].rearrange("p (n c) -> p n c", c=2),
                                              adab[:, layer, :].unsqueeze(2).to_broadcast([P, 6 * KD, 2]), ALU.add), t, t_in)
            free[key] = t
            for a in range(2):
                for c in range(2):
                    t2 = dve(lambda e: e.scalar_tensor_tensor(amp[:, a, :, c], mod[:, 3 * a + 1, :, c], 1.0, g2[:, layer, a, :], ALU.add, ALU.mult), t)
            free["cols"] = t2
            return t2

        def mod_row(which, c, dst, diag, *after):
            for half in range(2):
                bank, key = take_tr()
                for k in range(4):
                    kk = half * 4 + k
                    td = dve(lambda e: e.tensor_scalar(diag[:, k % 2, :], ident[:, :], mod[:, which, kk, c:c + 1], None, ALU.mult),
                             free.get(("diag", k % 2)), *after)
                    tp = pe(lambda e: e.matmul(bank[:, k * P:(k + 1) * P], ones[:, :], diag[:, k % 2, :], start=True, stop=True), td, free.get(key))
                    free[("diag", k % 2)] = tp
                t = act(lambda e: e.activation(dst[:, half * 512:(half + 1) * 512], bank[:, :], ACT.Copy), tp)
                free[key] = t
            return t

        def norm_all(a, with_ctx, scratch, tmp):
            t = normed_to_T(x, NT, scratch, tmp, lambda k: amp[:, a, k, 0:1], lambda k: mod[:, 3 * a, k, 0:1], x_hi, x_lo, False)
            if with_ctx:
                t = normed_to_T(cx, NC, scratch, tmp, lambda k: amp[:, a, k, 1:2], lambda k: mod[:, 3 * a, k, 1:2], c_hi, c_lo, False, free["scratch"])
            return t

        def rotate(qk, nheads, tmp, *after):
            for i in range(NT):
                v = qk(i).rearrange("p h (a b c) -> p h a b c", a=2, b=2)
                w = tmp[:, i, 0:nheads * HD2].rearrange("p (h a b c) -> p h a b c", a=2, b=2, c=16)
                sv = sin2[:, i, :].rearrange("p (a b c) -> p a b c", a=2, b=2)
                for b in range(2):
                    t = dve(lambda e: e.tensor_tensor(w[:, :, :, b, :], v[:, :, :, 1 - b, :],
                                                      sv[:, :, b, :].unsqueeze(1).to_broadcast([P, nheads, 2, 16]), ALU.mult), *after)
            for i in range(NT):
                t2 = dve(lambda e: e.tensor_tensor(qk(i), qk(i), cos2[:, i, :].unsqueeze(1).to_broadcast([P, nheads, HD2]), ALU.mult), t)
            for i in range(NT):
                t3 = dve(lambda e: e.tensor_tensor(qk(i), qk(i), tmp[:, i, 0:nheads * HD2].rearrange("p (h c) -> p h c", c=HD2), ALU.add), t2)
            return t3

        def mix_ab(y, th):
            st = contextlib.ExitStack()
            loc = lambda n, shape, dt=F32: sb_in(st, f"ab_{n}", shape, dt)
            NTC = NT + NC
            qk_raw = loc("qk_raw", [P, NTC, 2 * HD])
            vN = [loc(f"v{i}", [P, NTC, HD]) for i in range(2)]
            qT = [loc(f"qT{i}", [P, NTC * P]) for i in range(2)]
            kT = [loc(f"kT{i}", [P, NTC * P]) for i in range(2)]
            pr = [loc("pr0", [P, 768]), loc("pr1", [P, 14 * GRID_W])]
            probsT = loc("probsT", [P, 768])
            tmp = loc("tmp", [P, NT, 2 * HD])
            norm_scratch = tmp[:, :, :].rearrange("p i c -> p (i c)")[:, 0:NTC * HD].rearrange("p (i c) -> p i c", c=HD)
            lamv = tmp[:, 0, :].rearrange("p (a c) -> p a c", a=4)
            lam = loc("lam", [P, 4])
            subg = loc("subg", [P, HD])
            lam_init = 0.8 - 0.6 * math.exp(-0.3 * 0)
            load(subg[:, :], A["diff_sub_g_2"].to_broadcast([P, HD]), s_misc[5])
            tl = load(lamv, A["diff_lambda_2"].to_broadcast([P, 4, HD2]), s_misc[5])
            t = dve(lambda e: e.tensor_tensor(lamv[:, 0:4:2, :], lamv[:, 0:4:2, :], lamv[:, 1:4:2, :], ALU.mult), tl)
            t = dve(lambda e: e.tensor_reduce(lam[:, 0:2], lamv[:, 0:4:2, :], AX.X, ALU.add), t)
            t = act(lambda e: e.activation(lam[:, 0:2], lam[:, 0:2], ACT.Exp), t)
            t = dve(lambda e: e.tensor_tensor(lam[:, 2:3], lam[:, 1:2], lam[:, 0:1], ALU.subtract), t)
            t = dve(lambda e: e.tensor_scalar(lam[:, 2:3], lam[:, 2:3], -lam_init, None, ALU.add), t)
            t_lam = free["tmp"] = dve(lambda e: e.tensor_scalar(subg[:, :], subg[:, :], 1.0 - lam_init, None, ALU.mult), t)

            def project(u):
                b = u % 2
                n, wh, wl, ready = next_slab("ab")
                for i, (ah, al) in enumerate(x_tiles + c_tiles):
                    ps, key = take_proj()
                    for k in range(KD):
                        t = mm3(ps[:, 0:384], (ah(k), al(k)), (wh[:, k, :], wl[:, k, :]), k == 0, k == KD - 1, ready, th, free.get(key))
                    t1 = act(lambda e: e.activation(qk_raw[:, i, :], ps[:, 0:256], ACT.Copy), t, free.get("qk_raw"))
                    free[key] = act(lambda e: e.activation(vN[b][:, i, :], ps[:, 256:384], ACT.Copy), t, free.get(("head", b)))
                    pump()
                    if i == NTC - 1:
                        slab_done(n, t)
                        t2 = t1
                        if u < 4:
                            t2 = rotate(lambda i: qk_raw[:, i, :].rearrange("p (h c) -> p h c", c=HD2), 4, tmp, t1, free.get("tmp"))
                            free["tmp"] = t2
                        to_T(lambda i: qk_raw[:, i, 0:P], NTC, 0, qT[b][:, :], None, t1, t2, free.get(("head", b)))
                        free["qk_raw"] = to_T(lambda i: qk_raw[:, i, P:2 * P], NTC, 0, kT[b][:, :], None, t1, t2)
                        free[("qk", b)] = act.last()
                    yield

            def diff(u):
                b = u % 2
                for i in range(NTC):
                    k0, n = (0, 768) if i < NT else (S, CTX)
                    st4 = stats(8)
                    for a in range(2):
                        rows = slice(a * HD2, (a + 1) * HD2)
                        for c0 in range(0, n, 512):
                            w = min(512, n - c0)
                            t = pe(lambda e: e.matmul(score_ps[:, c0:c0 + w], qT[b][rows, i * P:(i + 1) * P], kT[b][rows, k0 + c0:k0 + c0 + w],
                                                      start=True, stop=True), free.get("scores"), free[("qk", b)])
                        mx, nm, den, rd = (st4[:, 4 * a + m:4 * a + m + 1] for m in range(4))
                        t = dve(lambda e: e.reduce_max(mx, score_ps[:, 0:n], AX.X), t)
                        t = dve(lambda e: e.tensor_scalar(nm, mx, -(HD2 ** -0.5), None, ALU.mult), t)
                        t = act(lambda e: e.activation(pr[a][:, 0:n], score_ps[:, 0:n], ACT.Exp, bias=nm, scale=HD2 ** -0.5, accum_out=den), t, free.get(("pr", a)))
                        free["scores"] = t
                        t = dve(lambda e: e.reciprocal(rd, den), t)
                        if a == 0:
                            t0 = dve(lambda e: e.tensor_scalar(pr[0][:, 0:n], pr[0][:, 0:n], rd, None, ALU.mult), t)
                            yield
                    t = dve(lambda e: e.tensor_tensor(rd, rd, lam[:, 2:3], ALU.mult), t, t_lam)
                    t = dve(lambda e: e.scalar_tensor_tensor(pr[0][:, 0:n], pr[1][:, 0:n], rd, pr[0][:, 0:n], ALU.mult, ALU.add), t, t0)
                    free[("pr", 1)] = t
                    yield
                    t = yield from transposed(pr[0], n, probsT, t)
                    free[("pr", 0)] = free["probs"]
                    j0 = k0 // P
                    t = weigh(probsT, n, [vN[b][:, j0 + j, :] for j in range(n // P)], HD, t)
                    dst = y[:, i, u * HD:(u + 1) * HD]
                    free["outp"] = act(lambda e: e.activation(dst, out_ps[:, 0:HD], ACT.Copy), t)
                    yield
                free[("head", b)] = t
                yv = y[:, :, u * HD:(u + 1) * HD]
                t = head_norms(yv, NTC, HD, norm_scratch, free["outp"], free.get("tmp"))
                free["tmp"] = dve(lambda e: e.tensor_tensor(yv, yv, subg[:, :].unsqueeze(1).to_broadcast([P, NTC, HD]), ALU.mult), t, t_lam)

            def neighbourhood(u):
                b = u % 2
                free["probs"] = [free.get("probs"), free.get(("pr", 0)), free.get(("pr", 1))]
                for a in range(2):
                    head = (u - 4) * 2 + a
                    rows = slice(a * HD2, (a + 1) * HD2)
                    bt = pr[1]
                    tb = load(bt[:, :], A["bias_tab"][head].rearrange("p j c -> p (j c)"), s_bias[0], free.get(("pr", 1)))
                    for i in range(NTC):
                        q = qT[b][rows, i * P:(i + 1) * P]
                        dst = y[:, i, DIFF_W + head * HD2:DIFF_W + (head + 1) * HD2]
                        if i < NT:
                            segs = [(kT[b][rows, 0:S], 0, S, None), (kT[b][rows, S:S + CTX], S, CTX, None)]
                            vals = [vN[b][:, j, rows] for j in range(NTC)]
                            o = (6 - 2 * i) * GRID_W
                            yield from attend(q, segs, 768, vals, HD2, HD2 ** -0.5, pr[0], probsT, scaled_into(dst),
                                              bias=(bt[:, o:o + S], tb), after=[free[("qk", b)]])
                            free[("pr", 1)] = free["scores"]
                        else:
                            segs = [(kT[b][rows, S:S + CTX], 0, CTX, None)]
                            vals = [vN[b][:, j, rows] for j in range(NT, NTC)]
                            yield from attend(q, segs, CTX, vals, HD2, HD2 ** -0.5, pr[0], probsT, scaled_into(dst), after=[free[("qk", b)]])
                free[("head", b)] = pe.last()

            for _ in project(0):
                pass
            for u in range(8):
                weave(project(u + 1) if u < 7 else iter(()), diff(u) if u < 4 else neighbourhood(u), 4)
            fence()
            st.close()

        def mix_c(y, th):
            st = contextlib.ExitStack()
            loc = lambda n, shape, dt=F32: sb_in(st, f"c_{n}", shape, dt)
            NTC = NT + NC
            band = loc("band", [P, 2, P], BF16)
            sinks = loc("sinks", [P, 16])
            raw_ = loc("qk_raw", [P, NTC, 384])
            vN = [loc(f"v{i}", [P, NTC, HD2]) for i in range(2)]
            qT = [loc(f"qT{i}", [P, 2, S]) for i in range(2)]
            kT = [loc(f"kT{i}", [P, NTC * P]) for i in range(2)]
            probs = loc("probs", [P, 640])
            probsT = loc("probsT", [P, 640])
            tmp = loc("tmp", [P, NT, 384])
            bandf = tmp[:, 0, 0:2 * P]
            load(sinks[:, :], A["attn_sinks_2"].to_broadcast([P, 16]), s_misc[6])
            tl = load(bandf, A["band"], s_misc[6])
            t = free["tmp"] = dve(lambda e: e.tensor_copy(band[:, :, :].rearrange("p a k -> p (a k)"), bandf), tl)
            free["masks"] = [t, free["const"]]

            def project(j):
                b = j % 2
                n, wh, wl, ready = next_slab("c")
                for i, (ah, al) in enumerate(x_tiles + c_tiles):
                    c0 = 0 if i < NT else 256
                    ps, key = take_proj()
                    for k in range(KD):
                        t = mm3(ps[:, c0:384], (ah(k), al(k)), (wh[:, k, c0:384], wl[:, k, c0:384]), k == 0, k == KD - 1, ready, th, free.get(key))
                    if i < NT:
                        act(lambda e: e.activation(raw_[:, i, 0:256], ps[:, 0:256], ACT.Copy), t, free.get("qk_raw"))
                    t1 = act(lambda e: e.activation(raw_[:, i, 256:384].rearrange("p (a c) -> p a c", a=2),
                                                    ps[:, 256:320].unsqueeze(1).to_broadcast([P, 2, HD2]), ACT.Copy), t, free.get("qk_raw"))
                    free[key] = act(lambda e: e.activation(vN[b][:, i, :], ps[:, 320:384], ACT.Copy), t, free.get(("head", b)))
                    pump()
                    if i == NTC - 1:
                        slab_done(n, t)
                        t2 = rotate(lambda i: raw_[:, i, :].rearrange("p (h c) -> p h c", c=HD2), 6, tmp, t1, free.get("tmp"))
                        free["tmp"] = t2
                        for a in range(2):
                            to_T(lambda i: raw_[:, i, a * P:(a + 1) * P], NT, 0, qT[b][:, a, :], None, t1, t2, free.get(("head", b)))
                        free["qk_raw"] = to_T(lambda i: raw_[:, i, 256:384], NTC, 0, kT[b][:, :], None, t1, t2, free.get(("head", b)))
                        free[("qk", b)] = act.last()
                    yield

            def attention(j):
                b = j % 2
                for hh in range(4):
                    head = j * 4 + hh
                    a, part = hh // 2, hh % 2
                    rows = slice(part * HD2, (part + 1) * HD2)
                    for i in range(NT):
                        blocks = [m for m in (i - 1, i, i + 1) if 0 <= m < NT] + [NT, NT + 1]
                        segs = []
                        for n_, m in enumerate(blocks):
                            mask = None if m >= NT or m == i else band[:, 0 if m < i else 1, :]
                            segs.append((kT[b][rows, m * P:(m + 1) * P], n_ * P, P, mask))
                        vals = [vN[b][:, m, :] for m in blocks]
                        yield from attend(qT[b][rows, a, i * P:(i + 1) * P], segs, len(blocks) * P, vals, HD2, HD2 ** -0.5, probs, probsT,
                                          scaled_into(y[:, i, head * HD2:(head + 1) * HD2]), sink=sinks[:, head:head + 1], after=[free[("qk", b)]])
                free[("head", b)] = pe.last()

            for _ in project(0):
                pass
            for j in range(4):
                weave(project(j + 1) if j < 3 else iter(()), attention(j), 8)
            fence()
            st.close()

        wide = proj_ps + tr_ps + [score_ps[:, 0:512], score_ps[:, 512:1024], out_ps]
        turn["wide"] = 0

        def take_wide():
            i = turn["wide"] % 8
            turn["wide"] += 1
            return wide[i], ("wide", i)

        def tail(layer, y, with_ctx, ls):
            tiles = x_tiles + (c_tiles if with_ctx else [])
            rows_of = lambda i: x[:, i, :] if i < NT else cx[:, i - NT, :]
            st = contextlib.ExitStack()
            loc = lambda n, shape, dt=F32: sb_in(st, f"t{layer}_{n}", shape, dt)
            row = [loc(f"row{c}", [P, D]) for c in range(2 if with_ctx else 1)]
            diag = loc("diag", [P, 2, P])
            gtmp = loc("gtmp", [P, 2, 512])
            rows_to_T(y[:, 0:NT, :], NT, KD, x_hi, x_lo, False)
            if with_ctx:
                rows_to_T(y[:, NT:NT + NC, :], NC, KD, c_hi, c_lo, False)
            th = dve.last()
            trow = [mod_row(2, c, row[c], diag) for c in range(len(row))]
            fence()
            for c0, c1 in COLS:
                n, wh, wl, ready = next_slab("out2")
                w = c1 - c0
                for i, (ah, al) in enumerate(tiles):
                    ps, key = take_wide()
                    for k in range(KD):
                        t = mm3(ps[:, 0:w], (ah(k), al(k)), (wh[:, k, :], wl[:, k, :]), k == 0, k == KD - 1, ready, free.get(key))
                    pump()
                    free[key] = add_gated(rows_of(i)[:, c0:c1], ps[:, 0:w], row[0 if i < NT else 1][:, c0:c1], gtmp, t)
                slab_done(n, t)
            fence()
            st.close()
            if stage == 3:
                ls.close()
                return
            with contextlib.ExitStack() as s1:
                tmp = sb_in(s1, f"t{layer}_tmp", [P, 2, 512])
                norm_all(1, with_ctx, y[:, 0:NT, :], tmp)
                fence()
            ls.close()
            st = contextlib.ExitStack()
            loc = lambda n, shape, dt=F32: sb_in(st, f"f{layer}_{n}", shape, dt)
            row = [loc(f"row{c}", [P, D]) for c in range(2 if with_ctx else 1)]
            diag = loc("diag", [P, 2, P])
            gtmp = loc("gtmp", [P, 2, 512])
            trow = [mod_row(5, c, row[c], diag) for c in range(len(row))]
            NTOK = S + (CTX if with_ctx else 0)
            gh = loc("gh", [P, 6, NTOK], F32R)
            gl = loc("gl", [P, 6, NTOK], F32R)
            fence()
            hs = loc("hs", [P, 2, S])
            for a, b in FPARTS:
                for j in range(a, b):
                    n, wh, wl, ready = next_slab("up")
                    for c0, width, hi_of, lo_of in ((0, S, x_hi, x_lo), (S, CTX, c_hi, c_lo))[0:2 if with_ctx else 1]:
                        pair = []
                        for part in range(2):
                            ps, key = take_wide()
                            for k in range(KD):
                                cs_ = slice(part * P, (part + 1) * P)
                                t = mm3(ps[:, 0:width], (wh[:, k, cs_], wl[:, k, cs_]), (hi_of(k), lo_of(k)), k == 0, k == KD - 1, ready, free.get(key))
                            pair.append((ps, key, t))
                            pump()
                        (pa, ka, ta), (pb, kb, tb) = pair
                        slot = turn.setdefault("hs", 0) % 2
                        turn["hs"] += 1
                        h_ = hs[:, slot, 0:width]
                        t1 = act(lambda e: e.activation(h_, pa[:, 0:width], ACT.Silu), ta, free.get(("hs", slot)))
                        free[ka] = t1
                        t1 = dve(lambda e: e.tensor_tensor(h_, h_, pb[:, 0:width], ALU.mult), t1, tb)
                        free[kb] = t1
                        gv = (slice(None), j - a, slice(c0, c0 + width))
                        t2 = act(lambda e: e.activation(gh[gv], h_, ACT.Copy), t1, free.get("gT"))
                        t3 = dve(lambda e: e.tensor_tensor(gl[gv], h_, gh[gv].bitcast(F32), ALU.subtract), t2)
                        free[("hs", slot)] = t3
                    slab_done(n, tb)
                for half in range(2):
                    n, wh, wl, ready = next_slab("down")
                    for i in range(len(tiles)):
                        ps, key = take_wide()
                        for k in range(b - a):
                            gv = (slice(None), k, slice(i * P, (i + 1) * P))
                            t = mm3(ps[:, 0:512], (gh[gv], gl[gv]), (wh[:, k, :], wl[:, k, :]), k == 0, k == b - a - 1, ready, t3, free.get(key))
                        pump()
                        cc = slice(half * 512, (half + 1) * 512)
                        free[key] = add_gated(rows_of(i)[:, cc], ps[:, :], row[0 if i < NT else 1][:, cc], gtmp, t)
                    slab_done(n, t)
                free["gT"] = t
            fence()
            st.close()

        def add_gated(dst, ps, row, gtmp, t):
            slot = turn.setdefault("gadd", 0) % 2
            turn["gadd"] += 1
            w = dst.shape[-1]
            m = gtmp[:, slot, 0:w]
            t = dve(lambda e: e.tensor_tensor(m, ps, row, ALU.mult), t, free.get(("gadd", slot)))
            free[("gadd", slot)] = pool(lambda e: e.tensor_tensor(dst, dst, m, ALU.add), t)
            return t

        for layer in range(2):
            ls = contextlib.ExitStack()
            y = sb_in(ls, f"s{layer}_y", [P, NT + NC, D])
            modulations(layer)
            with contextlib.ExitStack() as s0:
                tmp = sb_in(s0, f"s{layer}_tmp", [P, 2, 512])
                norm_all(0, True, y[:, 0:NT, :], tmp)
                fence()
            if layer == 0:
                mix_ab(y, None)
            else:
                mix_c(y, None)
            tail(layer, y, layer == 0, ls)
            if stage in (3, 4) and layer == 0:
                dump(x[:, :, :])
                ctxs.close()
                return
        with contextlib.ExitStack() as s1:
            fg = sb_in(s1, "fin_g", [P, D])
            o = sb_in(s1, "fin_o", [P, NT, D])
            tg = load(fg[:, :], A["final_g_2"].unsqueeze(0).to_broadcast([P, D]), s_misc[7])
            ss = stats(NT)
            for i in range(NT):
                t = act(lambda e: e.activation(o[:, i, :], x[:, i, :], ACT.Square, accum_out=ss[:, i:i + 1]))
            t = inv_rms(ss, D, t)
            for i in range(NT):
                t2 = dve(lambda e: e.scalar_tensor_tensor(o[:, i, :], x[:, i, :], ss[:, i:i + 1], fg[:, :], ALU.mult, ALU.mult), t, tg)
                load(out[0, i * P:(i + 1) * P, :], o[:, i, :], s_out, t2)
            sp.wait(s_out.token())
        ctxs.close()

    first_block_layer(0)
    if stage == 1:
        dump(x[:, :, :])
    if not finished["v"]:
        first_block_layer(1)
    if stage == 2:
        dump(x[:, :, :])
    if not finished["v"]:
        second_block()

    with nc.Block() as block:
        @block.sync
        def _(e):
            sp.emit(e)

        @block.tensor
        def _(e):
            pe.emit(e)

        @block.scalar
        def _(e):
            act.emit(e)

        @block.vector
        def _(e):
            dve.emit(e)

        @block.gpsimd
        def _(e):
            pool.emit(e)
    ctx.close()


def arrays_of(inputs):
    a = {k: np.ascontiguousarray(v) for k, v in inputs.items()}
    c = dict(shape_constants())
    cols = lambda v: np.ascontiguousarray(np.asarray(v).reshape(-1, KD, P).transpose(2, 0, 1)).reshape(P, -1)
    c["gain_cols"] = np.concatenate([cols(a["norm_gain"]), cols(a["mem_norm_gain"]), cols(a["norm_g_2"][:, 0])], 1)
    c["gain_cols_2"] = cols(a["norm_g_2"])
    c["c_cols"] = np.concatenate([cols(a["c_2"]), cols(a["c_ctx_2"])], 1)
    c["ada_b_cols"] = cols(a["ada_b_2"])
    c["lb_cols"] = cols(a["lb_logits"])
    g = np.concatenate([a["q_gain_a"][0], a["k_gain_a"][0]], 0).T.copy()
    g[:ROT] = 1.0
    c["gain_a_cols"] = g
    c["bias_tab"] = bias_table(a.pop("na_rpb_2")[0])
    a.pop("norm_gain"), a.pop("mem_norm_gain"), a.pop("lb_logits"), a.pop("norm_g_2")
    a.pop("c_2"), a.pop("c_ctx_2"), a.pop("ada_b_2")
    return {**a, **c}


def declare(nc, arrays, stage=99):
    aps = {n: nc.dram_tensor(f"in_{n}", v.shape, mybir.dt.from_np(v.dtype), kind="ExternalInput").ap() for n, v in arrays.items()}
    out = nc.dram_tensor("out", (1, S, D), F32, kind="ExternalOutput").ap()
    build(nc, aps, out, stage)


def kernel(**inputs):
    import concourse.bacc as bacc
    from concourse.bass_utils import run_bass_kernel_spmd
    arrays = arrays_of(inputs)
    nc = bacc.Bacc("TRN2", target_bir_lowering=False, num_devices=1)
    declare(nc, arrays)
    r = run_bass_kernel_spmd(nc, [{f"in_{n}": v for n, v in arrays.items()}], core_ids=[0])
    return r.results[0]["out"]
```

```python
import contextlib
import math

import numpy as np
import concourse.bass as bass
from concourse import mybir

F32 = mybir.dt.float32
F32R = mybir.dt.float32r
BF16 = mybir.dt.bfloat16
I32 = mybir.dt.int32
ALU = mybir.AluOpType
ACT = mybir.ActivationFunctionType
AX = mybir.AxisListType

P = 128
D = 1024
KD = D // P
S = 512
NT = S // P
CTX = 256
NC = CTX // P
HD = 128
AH = 8
NG = 3
DILS = (1, 4, 16)
BACK = 128
ROT = 32
HALF = ROT // 2
MH = 4
MEMW = MH * HD
MIX = AH * HD + MEMW
HD2 = 64
GRID_W = 64
NA_R = 8
NA_C = 16
FFN = 2816
KF = FFN // P
NEG = -1e30
EPS = 1e-6
CHUNK = 128
LEVELS = (64, 32, 16, 8, 4, 2, 1)
SLAB = 3072
PIECE = 1536
RES = 4


def shape_constants():
    c = {}
    c["ident"] = np.eye(P, dtype=np.float32)
    pos = np.arange(S).reshape(P, RES).T
    mask = np.zeros((P, RES, 768), np.float32)
    for r in range(RES):
        q = pos[r][:, None]
        k0 = pos.reshape(-1)[None, :]
        kr = pos[r][None, :]
        for sl, k, dil in ((slice(0, 512), k0, 1), (slice(512, 640), kr, 4), (slice(640, 768), kr, 16)):
            dist = q - k
            ok = (dist >= 0) & (dist <= dil * BACK) & (dist % dil == 0)
            mask[:, r, sl] = np.where(ok, 0.0, NEG)
    c["mask_a"] = mask.reshape(P, RES * 768)
    inv = (np.float32(500000.0) ** (-np.arange(0, ROT, 2, dtype=np.float32) / np.float32(ROT))).astype(np.float32)
    c["inv_freq"] = np.broadcast_to(inv, (P, HALF)).copy()
    carry = np.ones((P, S), np.float32)
    carry[:, ::CHUNK] = 0.0
    c["carry"] = carry
    lm = np.zeros((P, 8, P), np.float32)
    s_, t_ = np.arange(P)[:, None], np.arange(P)[None, :]
    for n, L in enumerate(LEVELS):
        lm[:, n] = (s_ // (2 * L) == t_ // (2 * L)) & ((s_ // L) % 2 == 0) & ((t_ // L) % 2 == 1)
    lm[:, 7] = s_ == t_
    c["level_mask"] = lm.reshape(P, 1024)
    t = np.arange(S)
    quarter = HD2 // 4
    invq = (np.float32(10000.0) ** (-np.arange(quarter, dtype=np.float32) / np.float32(quarter))).astype(np.float32)
    ar = (t // GRID_W).astype(np.float32)[:, None] * invq
    ac = (t % GRID_W).astype(np.float32)[:, None] * invq
    ang = np.concatenate([ar, ar, ac, ac], -1)
    sign = np.tile(np.repeat(np.array([-1.0, 1.0], np.float32), quarter), 2)
    c["cos2"] = np.cos(ang).astype(np.float32)
    c["sin2"] = (np.sin(ang).astype(np.float32) * sign).astype(np.float32)
    i_, j_ = np.arange(P)[:, None], np.arange(P)[None, :]
    c["band"] = np.concatenate([np.where(j_ >= i_, 0.0, NEG), np.where(j_ <= i_, 0.0, NEG)], 1).astype(np.float32)
    return c


def bias_table(rpb):
    col = np.arange(GRID_W)
    start = np.clip(col - NA_C // 2, 0, GRID_W - NA_C)
    kc = col[None, :]
    ok = (kc >= start[:, None]) & (kc < start[:, None] + NA_C)
    dc = np.clip(kc - col[:, None] + NA_C - 1, 0, 2 * NA_C - 2)
    wide = rpb[:, :, dc]
    wide = np.where(ok[None, None], wide, np.float32(NEG)).astype(rpb.dtype)
    wide = wide.transpose(0, 2, 1, 3)
    return np.ascontiguousarray(np.concatenate([wide[:, :, 1:15], wide[:, :, 0:14]], axis=1))


class Noted:

    def matmul(self, *a, **k):
        return lambda e: e.matmul(*a, **k)

    def transpose(self, *a, **k):
        return lambda e: e.transpose(*a, **k)

    def activation(self, *a, **k):
        return lambda e: e.activation(*a, **k)

    def tensor_tensor(self, *a, **k):
        return lambda e: e.tensor_tensor(*a, **k)

    def tensor_scalar(self, *a, **k):
        return lambda e: e.tensor_scalar(*a, **k)

    def scalar_tensor_tensor(self, *a, **k):
        return lambda e: e.scalar_tensor_tensor(*a, **k)

    def tensor_copy(self, *a, **k):
        return lambda e: e.tensor_copy(*a, **k)

    def tensor_reduce(self, *a, **k):
        return lambda e: e.tensor_reduce(*a, **k)

    def reduce_max(self, *a, **k):
        return lambda e: e.reduce_max(*a, **k)

    def reciprocal(self, *a, **k):
        return lambda e: e.reciprocal(*a, **k)

    def memset(self, *a, **k):
        return lambda e: e.memset(*a, **k)

    def tensor_tensor_scan(self, *a, **k):
        return lambda e: e.tensor_tensor_scan(*a, **k)


NOTED = Noted()


class Engine:

    def __init__(self, sem):
        self.sem, self.n, self.queue, self.waited = sem, 0, [], {}

    def wait(self, *tokens):
        for t in tokens:
            if t is None:
                continue
            if isinstance(t, list):
                self.wait(*t)
                continue
            sem, value = t
            if value > self.waited.get(sem.name, 0):
                self.waited[sem.name] = value
                self.queue.append(lambda e, s=sem, v=value: e.wait_ge(s, v))

    def __call__(self, fn, *after, signal=True):
        self.wait(*after)
        issue = fn(NOTED)
        if not signal:
            self.queue.append(issue)
            return None
        self.n += 1
        self.queue.append(lambda e: issue(e).then_inc(self.sem, 1))
        return (self.sem, self.n)

    def last(self):
        return (self.sem, self.n) if self.n else None

    def emit(self, e):
        for fn in self.queue:
            fn(e)


class Dma:

    def __init__(self, sem):
        self.sem, self.n = sem, 0

    def token(self):
        return (self.sem, self.n)


def weave(main, n_main, side, n_side):
    done = 0
    for m in range(n_main):
        if next(main, "end") == "end":
            break
        while done * n_main < (m + 1) * n_side:
            done += 1
            if next(side, "end") == "end":
                done = n_side
                break
    for _ in main:
        pass
    for _ in side:
        pass


LEAD = 2 * (KD + 1) + 4


def build(nc, A, out, stage=99):
    ctx = contextlib.ExitStack()
    sem = lambda n: ctx.enter_context(nc.semaphore(n))
    sb_in = lambda stack, n, shape, dt=F32: stack.enter_context(nc.sbuf_tensor(n, shape, dt))
    sb = lambda n, shape, dt=F32: sb_in(ctx, n, shape, dt)

    pe, act, dve, pool, sp = (Engine(sem(f"s_{n}")) for n in ("pe", "act", "dve", "pool", "sp"))

    def load(dst, src, dma, *after, eng=None):
        eng = eng or sp
        eng.wait(*after)
        dma.n += 16
        eng.queue.append(lambda e, s=dma.sem: e.dma_start(dst, src).then_inc(s, 16))
        return dma.token()

    x = sb("x", [P, NT, D])
    slab_hi = [sb(f"slab_hi{i}", [P, SLAB], F32R) for i in range(2)]
    slab_lo = [sb(f"slab_lo{i}", [P, SLAB], F32R) for i in range(2)]
    raw = [sb(f"raw{i}", [P, PIECE]) for i in range(3)]
    hx_hi = sb("hx_hi", [P, KD, S], F32R)
    hx_lo = sb("hx_lo", [P, KD, S], F32R)
    ident = sb("ident", [P, P])
    identb = sb("identb", [P, P], BF16)
    ones = sb("ones", [P, P])
    stat = sb("stat", [P, 384])
    gcol = sb("gcol", [P, 6, KD])
    cs = sb("cs", [P, 2, KD])
    csT = sb("csT", [P, KD, 2])
    adab = sb("adab", [P, 2, 6 * KD])
    mod = sb("mod", [P, 2, 6, KD, 2])
    first_scope = contextlib.ExitStack()
    gmem = sb_in(first_scope, "gmem", [P, 4, HD])
    psum = lambda n, shape: ctx.enter_context(nc.psum_tensor(n, shape, F32))
    proj_ps = [psum(f"proj{i}", [P, 512]) for i in range(2)]
    score_ps = [psum(f"scores{i}", [P, 1024]) for i in range(2)]
    tr_ps = psum("tr", [P, 512])
    out_ps = psum("outp", [P, 512])
    banks = proj_ps + [s_[:, h * 512:(h + 1) * 512] for s_ in score_ps for h in range(2)] + [tr_ps, out_ps]
    free = {}
    turn = {"proj": 0, "wide": 0, "stat": 0, "unit": 0}

    def take_proj():
        i = turn["proj"] % 2
        turn["proj"] += 1
        return banks[i], i

    def idle_proj():
        i = turn["proj"] % 2
        return banks[i], i

    def take_wide():
        i = turn["wide"] % 8
        turn["wide"] += 1
        return banks[i], i

    def stats(n):
        if turn["stat"] + n > 384:
            turn["stat"] = 0
        a = turn["stat"]
        turn["stat"] += n
        return stat[:, a:a + n]

    s_const = Dma(sem("d_const"))
    s_raw = [Dma(sem(f"d_raw{i}")) for i in range(3)]
    s_x = Dma(sem("d_x"))
    s_misc = [Dma(sem(f"d_misc{i}")) for i in range(8)]
    s_bias = [Dma(sem(f"d_bias{i}")) for i in range(2)]
    s_out = Dma(sem("d_out"))

    jobs = []
    order = []

    def job(name, K, N, segments, per=None):
        per = per or max(1, PIECE // N)
        pieces = []
        for k0 in range(0, K, per):
            k1 = min(K, k0 + per)
            pieces.append((k0, k1, [(c, w, src[k0 * P:k1 * P, :].rearrange("(k p) n -> p k n", p=P))
                                    for c, w, src in segments]))
        jobs.append((name, K, N, pieces))

    wa, wb = A["w_in_a"][0], A["w_in_b"][0]
    AQ = NG * AH * HD
    for h in range(AH):
        for g in range(NG):
            job("a", KD, 384, [(t * 128, 128, wa[:, t * AQ + (g * AH + h) * HD:][:, 0:128]) for t in range(3)])

    def mem_and_out_jobs(layer, w, base, w_out):
        kv = A["w_mem_kv"][layer]
        for m in range(MH):
            job("mkv", KD, 256, [(0, 128, kv[:, m * HD:(m + 1) * HD]), (128, 128, kv[:, MEMW + m * HD:MEMW + (m + 1) * HD])])
        job("mq", KD, 256, [(0, 256, w[:, base:base + 256])])
        job("mq", KD, 256, [(0, 256, w[:, base + 256:base + 512])])
        for n in range(MIX // 384):
            job("gate", KD, 384, [(0, 384, w[:, base + MEMW + n * 384:base + MEMW + (n + 1) * 384])])
        for n in range(4):
            job("out", MIX // P, 256, [(0, 256, w_out[:, n * 256:(n + 1) * 256])])

    mem_and_out_jobs(0, wa, 3 * AQ, A["w_out_a"][0])
    for h in range(AH):
        job("b", KD, 384, [(t * 128, 128, wb[:, t * D + h * HD:t * D + (h + 1) * HD]) for t in range(3)])
    mem_and_out_jobs(1, wb, 3 * D, A["w_out_b"][0])
    DIFF_W = 512

    wab = A["w_in_ab_2"][0]
    for base_q, base_k, base_v in ((0, 1024, 1536), (512, 2048, 2560)):
        for p in range(4):
            job("ab", KD, 384, [(n * 128, 128, wab[:, b + p * 128:b + (p + 1) * 128])
                                for n, b in enumerate((base_q, base_k, base_v))])

    COLS = ((0, 384), (384, 768), (768, 1024))

    def tail_jobs(layer, w_out):
        for c0, c1 in COLS:
            job("out2", KD, c1 - c0, [(0, c1 - c0, w_out[:, c0:c1])])
        w1, w3, w2 = A["ffn_w1_2"][layer], A["ffn_w3_2"][layer], A["ffn_w2_2"][layer]
        for a, b in FPARTS:
            for j in range(a, b):
                job("up", KD, 256, [(0, 128, w1[:, j * P:(j + 1) * P]), (128, 128, w3[:, j * P:(j + 1) * P])], per=4)
            for n in range(2):
                job("down", b - a, 512, [(0, 512, w2[a * P:b * P, n * 512:(n + 1) * 512])])

    FPARTS = ((0, 6), (6, 12), (12, 17), (17, 22))
    tail_jobs(0, A["w_out_ab_2"][0])
    wc = A["w_in_c_2"][0]
    for j in range(4):
        job("c", KD, 384, [(0, 256, wc[:, j * 256:(j + 1) * 256]), (256, 64, wc[:, D + j * 64:D + (j + 1) * 64]),
                           (320, 64, wc[:, D + 256 + j * 64:D + 256 + (j + 1) * 64])])
    tail_jobs(1, A["w_out_c_2"][0])

    order += [(0, 0), (0, 1)]
    for n in range(AH * NG):
        order += [(None, 4 * n), (n + 1, 0), (None, 4 * n + 1), (None, 4 * n + 2), (n + 1, 1), (None, 4 * n + 3)]
    order += [(n, i) for n in range(AH * NG + 1, len(jobs)) for i in range(len(jobs[n][3]))]
    state = {"loaded": 0, "taken": 0, "slab": 0}
    pieces_split = [0] * len(jobs)
    raw_free = [None] * 3
    slab_free = [None] * 2
    slab_ready = {}
    piece_arrived = {}

    def load_piece():
        m = state["loaded"]
        if m >= len(order):
            return
        n, i = order[m]
        if n is None:
            view = raw[m % 3][:, 0:KD * P].rearrange("p (k n) -> p k n", n=P)
            src = A["ada_w_2"][i // 48][:, (i % 48) * P:(i % 48 + 1) * P].rearrange("(k p) n -> p k n", p=P)
            tok = load(view, src, s_raw[m % 3], raw_free[m % 3])
        else:
            _, K, N, ps = jobs[n]
            k0, k1, segs = ps[i]
            view = raw[m % 3][:, 0:(k1 - k0) * N].rearrange("p (k n) -> p k n", n=N)
            for c, w, src in segs:
                tok = load(view[:, :, c:c + w], src, s_raw[m % 3], raw_free[m % 3])
        piece_arrived[m] = tok
        state["loaded"] += 1

    def split_piece():
        m = state["taken"]
        n, i = order[m]
        _, K, N, ps = jobs[n]
        k0, k1, _ = ps[i]
        a, b = k0 * N, k1 * N
        src = raw[m % 3][:, 0:b - a]
        hi, lo = slab_hi[n % 2][:, a:b], slab_lo[n % 2][:, a:b]
        t_hi = act(lambda e: e.activation(hi, src, ACT.Copy), piece_arrived[m], slab_free[n % 2])
        t_lo = dve(lambda e: e.tensor_tensor(lo, src, hi.bitcast(F32), ALU.subtract), t_hi, piece_arrived[m])
        raw_free[m % 3] = [t_hi, t_lo]
        slab_ready[n] = [t_hi, t_lo]
        pieces_split[n] += 1
        state["taken"] += 1
        load_piece()

    def pump():
        m = state["taken"]
        if m < len(order) and order[m][0] is not None and order[m][0] <= state["slab"]:
            split_piece()

    def next_slab(name):
        n = state["slab"]
        _, K, N, ps = jobs[n]
        assert jobs[n][0] == name, (jobs[n][0], name)
        while pieces_split[n] < len(ps):
            split_piece()
        state["slab"] += 1
        hi = slab_hi[n % 2][:, 0:K * N].rearrange("p (k n) -> p k n", n=N)
        lo = slab_lo[n % 2][:, 0:K * N].rearrange("p (k n) -> p k n", n=N)
        return n, hi, lo, slab_ready[n]

    def direct_piece():
        m = state["taken"]
        assert order[m][0] is None
        state["taken"] += 1

        def done(token):
            raw_free[m % 3] = token
            load_piece()
        return order[m][1], raw[m % 3][:, 0:KD * P].rearrange("p (k n) -> p k n", n=P), piece_arrived[m], done

    def slab_done(n, token):
        slab_free[n % 2] = token

    def mm3(dst, lhs, rhs, first, last, *after):
        pe.wait(*after)
        (lh, ll), (rh, rl) = lhs, rhs
        pe(lambda e: e.matmul(dst, lh, rh, start=first, stop=False), signal=False)
        pe(lambda e: e.matmul(dst, lh, rl, start=False, stop=False), signal=False)
        return pe(lambda e: e.matmul(dst, ll, rh, start=False, stop=last), signal=last)

    def inv_rms(ss, width, *after):
        n = ss.shape[-1]
        half, y, a = stats(n), stats(n), stats(n)
        t = dve(lambda e: e.tensor_scalar(ss, ss, 1.0 / width, EPS, ALU.mult, ALU.add), *after)
        dve(lambda e: e.tensor_scalar(half, ss, -0.5, None, ALU.mult), t)
        t = dve(lambda e: e.tensor_scalar(a.bitcast(I32), ss.bitcast(I32), 1, None, ALU.logical_shift_right), t)
        t = dve(lambda e: e.tensor_scalar(y.bitcast(I32), a.bitcast(I32), -1.0, float(0x5F3759DF), ALU.mult, ALU.add), t)
        for step in range(3):
            t = dve(lambda e: e.tensor_tensor(a, y, y, ALU.mult), t)
            t = dve(lambda e: e.tensor_tensor(a, a, half, ALU.mult), t)
            t = dve(lambda e: e.scalar_tensor_tensor(ss if step == 2 else y, a, 1.5, y, ALU.add, ALU.mult), t)
        return t

    def normed_to_T(rows, ntiles, scratch, gain, shift, hi, lo, residue, *after):
        ss = stats(ntiles)
        for i in range(ntiles):
            t = act(lambda e, i=i: e.activation(scratch[:, i, :], rows[:, i, :], ACT.Square, accum_out=ss[:, i:i + 1]), *after)
        t = inv_rms(ss, D, t)
        for i in range(ntiles):
            t2 = dve(lambda e, i=i: e.tensor_scalar(scratch[:, i, :], rows[:, i, :], ss[:, i:i + 1], None, ALU.mult), t)
        w = ntiles * P
        for k in range(KD):
            bank, key = take_wide()
            for i in range(ntiles):
                tp = pe(lambda e, i=i: e.transpose(bank[:, i * P:(i + 1) * P], scratch[:, i, k * P:(k + 1) * P], ident[:, :]),
                        t2, free.get(key), free.get("const"), signal=(i == ntiles - 1))
            vi = (lambda ap: ap.rearrange("p (i r) -> p i r", r=RES)) if residue else (lambda ap: ap)
            vo = (lambda ap: ap.rearrange("p (r i) -> p i r", r=RES)) if residue else (lambda ap: ap)
            src = vi(bank[:, 0:w])
            t4 = act(lambda e, k=k: e.activation(vo(hi(k)), src, ACT.Identity, scale=gain(k), bias=shift(k) if shift else 0.0), tp, free.get("cols"), *after)
            t5 = dve(lambda e, k=k: e.scalar_tensor_tensor(vo(lo(k)), src, gain(k), vo(hi(k).bitcast(F32)), ALU.mult, ALU.subtract), t4)
            free[key] = t5
            if shift:
                t5 = dve(lambda e, k=k: e.tensor_scalar(lo(k), lo(k).bitcast(F32), shift(k), None, ALU.add), t5)
        free["scratch"] = tp
        return t5

    def rows_to_T(y, ntiles, nchunks, hi, lo, residue, *after):
        w = ntiles * P
        vi = (lambda ap: ap.rearrange("p (r i) -> p r i", r=RES)) if residue else (lambda ap: ap)
        vo = (lambda ap: ap.rearrange("p (i r) -> p r i", r=RES)) if residue else (lambda ap: ap)
        for k in range(nchunks):
            bank, key = take_wide()
            for i in range(ntiles):
                tp = pe(lambda e, i=i, k=k, bank=bank: e.transpose(bank[:, i * P:(i + 1) * P], y[:, i, k * P:(k + 1) * P], ident[:, :]),
                        free.get(key), *after, signal=(i == ntiles - 1))
            t4 = act(lambda e, k=k, bank=bank: e.activation(vo(hi(k)), vi(bank[:, 0:w]), ACT.Copy), tp, *after)
            t5 = dve(lambda e, k=k, bank=bank: e.tensor_tensor(vo(lo(k)), vi(bank[:, 0:w]), vo(hi(k).bitcast(F32)), ALU.subtract), t4)
            free[key] = t5
        return t5

    class Unit:

        def __init__(self, softmax, n, values, width, finish):
            self.softmax, self.n, self.values, self.width, self.finish = softmax, n, values, width, finish

    def pipeline(units, probs, probsT):
        def turn_over(u):
            for c0, (bank, at_), engine in ((0, (tr_ps, 6), dve), (512, idle_proj(), act)):
                c1 = min(c0 + 512, u.n)
                if c0 >= c1:
                    continue
                for c in range(c0, c1, P):
                    tp = pe(lambda e: e.transpose(bank[:, c - c0:c - c0 + P], u.probs[:, c:c + P], ident[:, :]),
                            u.ready, free.get(at_), signal=(c + P >= c1))
                dst, src = u.probsT[:, c0:c1], bank[:, 0:c1 - c0]
                after = (tp, free.get(("probsT", u.slot)))
                if engine is dve:
                    t = dve(lambda e: e.tensor_copy(dst, src), *after)
                else:
                    t = act(lambda e: e.activation(dst, src, ACT.Copy), *after)
                free[at_] = t
                u.turned.append(t)
            free[("probs", u.slot)] = tp

        def weigh(u):
            for j in range(u.n // P):
                t = pe(lambda e: e.matmul(out_ps[:, 0:u.width], u.probsT[:, j * P:(j + 1) * P], u.values[j], start=(j == 0), stop=(j == u.n // P - 1)),
                       u.turned, free.get(7), signal=(j == u.n // P - 1))
            free[("probsT", u.slot)] = t
            free[7] = u.finish(u, out_ps[:, 0:u.width], t)

        live = []
        for n in range(len(units) + 2):
            if n < len(units):
                u = units[n]
                u.slot = turn["unit"] % 2
                turn["unit"] += 1
                u.probs, u.probsT, u.turned = probs[u.slot], probsT[u.slot], []
                softmax = u.softmax(u)
                next(softmax)
                yield
            if 1 <= n <= len(units):
                turn_over(units[n - 1])
                yield
            if n < len(units):
                for _ in softmax:
                    pass
            if 2 <= n:
                weigh(units[n - 2])
                yield

    def take_scores():
        i = turn.setdefault("scores", 0) % 2
        turn["scores"] += 1
        return score_ps[i], 2 + 2 * i, [free.get(2 + 2 * i), free.get(3 + 2 * i)]

    def scores_read(b, token):
        free[b] = free[b + 1] = token

    def plain_unit(q, segments, n, values, width, scale, dst, sink=None, bias=None, after=lambda: ()):
        def softmax(u):
            u.stats = stats(5)
            mx, nm, den, rden, es = (u.stats[:, i:i + 1] for i in range(5))
            sc, b, sfree = take_scores()
            pe.wait(*sfree)
            pe.wait(*after())
            for kT, c, w, mask in segments:
                last = mask is None
                t = pe(lambda e: e.matmul(sc[:, c:c + w], q, kT, start=True, stop=last), signal=last)
                if mask is not None:
                    t = pe(lambda e: e.matmul(sc[:, c:c + w], identb[:, :], mask, start=False, stop=True), free.get("masks"))
            yield
            pfree = free.get(("probs", u.slot))
            if bias is None:
                t = dve(lambda e: e.reduce_max(mx, sc[:, 0:n], AX.X), t)
                if sink is None:
                    t = dve(lambda e: e.tensor_scalar(nm, mx, -scale, None, ALU.mult), t)
                else:
                    t = dve(lambda e: e.scalar_tensor_tensor(mx, mx, scale, sink, ALU.mult, ALU.max), t)
                    t = dve(lambda e: e.tensor_scalar(nm, mx, -1.0, None, ALU.mult), t)
                t = act(lambda e: e.activation(u.probs[:, 0:n], sc[:, 0:n], ACT.Exp, bias=nm, scale=scale, accum_out=den), t, pfree)
                scores_read(b, t)
            else:
                btab, btok = bias()
                t = dve(lambda e: e.scalar_tensor_tensor(u.probs[:, 0:512], sc[:, 0:512], scale, btab, ALU.mult, ALU.add), t, btok, pfree)
                free["bias"] = t
                t = dve(lambda e: e.tensor_scalar(u.probs[:, 512:n], sc[:, 512:n], scale, None, ALU.mult), t)
                scores_read(b, t)
                t = dve(lambda e: e.reduce_max(mx, u.probs[:, 0:n], AX.X), t)
                t = dve(lambda e: e.tensor_scalar(nm, mx, -1.0, None, ALU.mult), t)
                t = act(lambda e: e.activation(u.probs[:, 0:n], u.probs[:, 0:n], ACT.Exp, bias=nm, accum_out=den), t)
            u.ready = u.summed = t
            if sink is not None:
                u.summed = act(lambda e: e.activation(es, sink, ACT.Exp, bias=nm), t)

        def finish(u, o, t):
            mx, nm, den, rden, es = (u.stats[:, i:i + 1] for i in range(5))
            td = u.summed
            if sink is not None:
                td = dve(lambda e: e.tensor_tensor(den, den, es, ALU.add), td)
            td = dve(lambda e: e.reciprocal(rden, den), td)
            return act(lambda e: e.activation(dst, o, ACT.Copy, scale=rden), t, td)

        return Unit(softmax, n, values, width, finish)

    pending = []

    def to_T(raw_ap, tiles, dst, scale_col, after, done=None):
        def part(b0, b1):
            def go():
                bank, key = idle_proj()
                for i in range(b0, b1):
                    tp = pe(lambda e: e.transpose(bank[:, (i - b0) * P:(i - b0 + 1) * P], raw_ap(i), ident[:, :]),
                            free.get(key), *after(), signal=(i == b1 - 1))
                src, d = bank[:, 0:(b1 - b0) * P], dst[:, b0 * P:b1 * P]
                if scale_col is None:
                    t = act(lambda e: e.activation(d, src, ACT.Copy), tp, *after())
                else:
                    t = dve(lambda e: e.tensor_scalar(d, src, scale_col, None, ALU.mult), tp, *after())
                free[key] = t
                if b1 == tiles and done:
                    done([tp, t])
            return go
        for b0 in range(0, tiles, 4):
            pending.append(part(b0, min(tiles, b0 + 4)))

    def flush():
        while pending:
            pending.pop(0)()

    def product(lhs, rhs, n_k, width, evacuate, *after, at=()):
        ps, key = take_proj()
        for k in range(n_k):
            if k in at and pending:
                pending.pop(0)()
            t = mm3(ps[:, width], lhs(k), rhs(k), k == 0, k == n_k - 1, *after, free.get(key))
            yield
        free[key] = evacuate(ps, t)
        return t

    def head_norms(view, nheads, width, sq, *after, eng=None):
        ss = stats(nheads)
        t = act(lambda e: e.activation(sq, view, ACT.Square), *after)
        t = dve(lambda e: e.tensor_reduce(ss, sq, AX.X, ALU.add), t)
        t = inv_rms(ss, width, t)
        return (eng or dve)(lambda e: e.tensor_tensor(view, view, ss.unsqueeze(2).to_broadcast([P, nheads, width]), ALU.mult), t)

    t_x = load(x[:, :, :], A["x"][0].rearrange("(i p) d -> p i d", p=P), s_x)
    for _ in range(3):
        load_piece()
    load(ident[:, :], A["ident"], s_const)
    load(gcol[:, 0:6, :], A["gain_cols"].rearrange("p (n k) -> p n k", k=KD), s_const)
    for n in range(2):
        load(gmem[:, n, :], A["mem_q_gain"][n:n + 1, :].to_broadcast([P, HD]), s_const)
        load(gmem[:, 2 + n, :], A["mem_k_gain"][n:n + 1, :].to_broadcast([P, HD]), s_const)
    load(cs[:, :, :], A["c_cols"].rearrange("p (a k) -> p a k", k=KD), s_const)
    load(adab[:, :, :], A["ada_b_cols"].rearrange("p (l n) -> p l n", l=2), s_const)
    t_const = s_const.token()
    free["cols"] = t_const
    t = act(lambda e: e.activation(cs[:, :, :], cs[:, :, :], ACT.Silu), t_const)
    free["cs"] = [t_const, dve(lambda e: e.tensor_copy(csT[:, :, :], cs[:, :, :].rearrange("p a k -> p k a")), t)]
    free["ones"] = dve(lambda e: e.memset(ones[:, :], 1.0))
    free["const"] = [t_const, dve(lambda e: e.tensor_copy(identb[:, :], ident[:, :]), t_const)]
    all_done = lambda: [pe.last(), act.last(), dve.last(), pool.last()]

    def fence():
        toks = all_done()
        for e in (pe, act, dve, pool):
            e.wait(*toks)
        free["stage"] = toks

    x_hi, x_lo = (lambda k: hx_hi[:, k, :]), (lambda k: hx_lo[:, k, :])
    finished = {"v": False}

    def dump(view):
        fence()
        sp.wait(*free["stage"])
        load(out[0].rearrange("(i p) d -> p i d", p=P), view, s_out)
        sp.wait(s_out.token())
        finished["v"] = True

    def ada_chunk():
        n, w, arrived, done = direct_piece()
        ps, key = take_proj()
        for k in range(KD):
            t = pe(lambda e: e.matmul(ps[:, 0:2], w[:, k, :], csT[:, k, :], start=(k == 0), stop=(k == KD - 1)),
                   arrived, free["cs"], free.get(key), signal=(k == KD - 1))
        done(t)
        layer, c = n // 48, n % 48
        free[key] = free["mod"] = dve(lambda e: e.tensor_scalar(mod[:, layer, c // KD, c % KD, :], ps[:, 0:2], adab[:, layer, c:c + 1], None, ALU.add),
                                      t, free["cs"])

    def first_block_layer(layer):
        st = contextlib.ExitStack()
        loc = lambda n, shape, dt=F32: sb_in(st, f"l{layer}_{n}", shape, dt)
        ymix = loc("ymix", [P, NT, D])
        ymem = loc("ymem", [P, NT, MEMW])
        heads = dilated_heads(ymix, ymem) if layer == 0 else gated_heads(ymix)
        if layer == 0:
            next(heads)
        free["hx"] = normed_to_T(x, NT, ymix, lambda k: gcol[:, layer, k:k + 1], None, x_hi, x_lo, layer == 0, t_x)
        for _ in heads:
            pass
        fence()
        s1 = contextlib.ExitStack()
        m1 = lambda n, shape, dt=F32: sb_in(s1, f"m{layer}_{n}", shape, dt)
        sg = m1("sg", [P, 2, 384])
        kmT = m1("kmT", [P, MH, CTX])
        vm = m1("vm", [P, NC, MH, HD])
        sq = m1("sq", [P, NT, 2, HD])
        qraw = [m1(f"qraw{i}", [P, NT, 2, HD]) for i in range(2)]
        kraw = qraw[1][:, :, :, :].rearrange("p (i n) a d -> p i (n a) d", n=2)
        qT = [m1(f"qT{i}", [P, 2, S]) for i in range(2)]
        probs = [m1(f"probs{i}", [P, CTX]) for i in range(2)]
        probsT = [m1(f"probsT{i}", [P, CTX]) for i in range(2)]
        s2 = contextlib.ExitStack()
        memx = sb_in(s2, f"m{layer}_memx", [P, NC, D])
        m_hi = sb_in(s2, f"m{layer}_hi", [P, KD, CTX], F32R)
        m_lo = sb_in(s2, f"m{layer}_lo", [P, KD, CTX], F32R)
        t_mem = load(memx[:, :, :], A["mem"][0].rearrange("(i p) d -> p i d", p=P), s_misc[0], free["stage"])
        mscr = ymem[:, :, :].rearrange("p i c -> p (i c)").rearrange("p (i c) -> p i c", c=D)

        def mem_keys():
            th = normed_to_T(memx, NC, mscr, lambda k: gcol[:, 2 + layer, k:k + 1], None,
                             lambda k: m_hi[:, k, :], lambda k: m_lo[:, k, :], False, t_mem)
            for m in range(MH):
                n, wh, wl, ready = next_slab("mkv")
                for i in range(NC):
                    def evacuate(ps, t):
                        act(lambda e: e.activation(kraw[:, i, m, :], ps[:, 0:128], ACT.Copy), t)
                        return act(lambda e: e.activation(vm[:, i, m, :], ps[:, 128:256], ACT.Copy), t)
                    ts = slice(i * P, (i + 1) * P)
                    t = yield from product(lambda k: (m_hi[:, k, ts], m_lo[:, k, ts]), lambda k: (wh[:, k, :], wl[:, k, :]), KD, slice(0, 256), evacuate, ready, th)
                    pump()
                slab_done(n, t)
            k8 = kraw.rearrange("p i m d -> p (i m) d")
            t = head_norms(k8, NC * MH, HD, sq[:, :, :, :].rearrange("p i a d -> p (i a) d"), act.last())
            t = dve(lambda e: e.tensor_tensor(k8, k8, gmem[:, 2 + layer, :].unsqueeze(1).to_broadcast([P, NC * MH, HD]), ALU.mult), t)
            for m in range(MH):
                to_T(lambda i, m=m: kraw[:, i, m, :], NC, kmT[:, m, :], None, lambda: [t])
            free["sq"] = t

        def mem_queries(half):
            n, wh, wl, ready = next_slab("mq")
            for i in range(NT):
                def evacuate(ps, t):
                    return act(lambda e: e.activation(qraw[half][:, i, :, :].rearrange("p a d -> p (a d)"), ps[:, 0:256], ACT.Copy), t)
                ts = slice(i * P, (i + 1) * P)
                t = yield from product(lambda k: (hx_hi[:, k, ts], hx_lo[:, k, ts]), lambda k: (wh[:, k, :], wl[:, k, :]), KD, slice(0, 256), evacuate, ready)
                pump()
                if i >= 1:
                    flush()
            slab_done(n, t)
            q8 = qraw[half][:, :, :, :].rearrange("p i a d -> p (i a) d")
            tq = head_norms(q8, 2 * NT, HD, sq[:, :, :, :].rearrange("p i a d -> p (i a) d"), act.last(), free.get("sq"))
            tq = free["sq"] = dve(lambda e: e.tensor_tensor(q8, q8, gmem[:, layer, :].unsqueeze(1).to_broadcast([P, 2 * NT, HD]), ALU.mult), tq)
            for a in range(2):
                to_T(lambda i, a=a: qraw[half][:, i, a, :], NT, qT[half][:, a, :], None, lambda: [tq])

        def gate(c0, c1):
            for c in range(c0, c1):
                n, wh, wl, ready = next_slab("gate")
                for i in range(NT):
                    def evacuate(ps, t):
                        slot = turn.setdefault("sg", 0) % 2
                        turn["sg"] += 1
                        g = sg[:, slot, :]
                        t1 = act(lambda e: e.activation(g, ps[:, 0:384], ACT.Silu), t, free.get(("sg", slot)))
                        for a, b, y, off in ((0, D, ymix, 0), (D, MIX, ymem, D)):
                            lo_, hi_ = max(a, c * 384), min(b, (c + 1) * 384)
                            if lo_ < hi_:
                                yv = y[:, i, lo_ - off:hi_ - off]
                                t2 = dve(lambda e: e.tensor_tensor(yv, yv, g[:, lo_ - c * 384:hi_ - c * 384], ALU.mult), t1, free.get("mem done"))
                        free[("sg", slot)] = t2
                        return t1
                    ts = slice(i * P, (i + 1) * P)
                    t = yield from product(lambda k: (hx_hi[:, k, ts], hx_lo[:, k, ts]), lambda k: (wh[:, k, :], wl[:, k, :]), KD, slice(0, 384), evacuate, ready)
                    pump()
                    if i >= 1:
                        flush()
                slab_done(n, t)

        for _ in mem_keys():
            pass
        for half in range(2):
            for _ in mem_queries(half):
                pass
        units = [plain_unit(qT[m // 2][:, m % 2, i * P:(i + 1) * P], [(kmT[:, m, :], 0, CTX, None)], CTX, [vm[:, j, m, :] for j in range(NC)],
                            HD, HD ** -0.5, ymem[:, i, m * HD:(m + 1) * HD], after=lambda: [free["mem T"]])
                 for m in range(MH) for i in range(NT)]

        def gate_then(c0, c1):
            first = gate(c0, c1)
            for _ in range(17):
                next(first)
            flush()
            free["mem T"] = act.last()
            return first
        rest = gate_then(0, 2)
        weave(rest, 47, pipeline(units, probs, probsT), 48)
        free["mem done"] = act.last()
        for _ in gate(2, 4):
            pass
        fence()
        s2.close()
        s1.close()
        s3 = contextlib.ExitStack()
        y_hi = sb_in(s3, f"o{layer}_hi", [P, 4, S], F32R)
        y_lo = sb_in(s3, f"o{layer}_lo", [P, 4, S], F32R)
        th = rows_to_T(ymix, NT, KD, x_hi, x_lo, layer == 0)
        th = rows_to_T(ymem, NT, 4, lambda k: y_hi[:, k, :], lambda k: y_lo[:, k, :], layer == 0)
        yh = lambda k: hx_hi[:, k, :] if k < KD else y_hi[:, k - KD, :]
        yl = lambda k: hx_lo[:, k, :] if k < KD else y_lo[:, k - KD, :]
        for c in range(4):
            n, wh, wl, ready = next_slab("out")
            for i in range(NT):
                ps, key = take_wide()
                ts = slice(i * P, (i + 1) * P)
                for k in range(MIX // P):
                    t = mm3(ps[:, 0:256], (yh(k)[:, ts], yl(k)[:, ts]), (wh[:, k, :], wl[:, k, :]), k == 0, k == MIX // P - 1, ready, th, free.get(key))
                pump()
                xv = x[:, i, c * 256:(c + 1) * 256]
                free[key] = dve(lambda e: e.tensor_tensor(xv, xv, ps[:, 0:256], ALU.add), t)
            slab_done(n, t)
        fence()
        s3.close()
        st.close()

    def dilated_heads(y, ymem):
        st = contextlib.ExitStack()
        loc = lambda n, shape, dt=F32: sb_in(st, f"a_{n}", shape, dt)
        masks = loc("masks", [P, RES, 768], BF16)
        qk_raw = [loc(f"qk_raw{i}", [P, NT, 2, HD]) for i in range(2)]
        qT = [loc(f"qT{i}", [P, NG, S]) for i in range(2)]
        kT = [loc(f"kT{i}", [P, NG, S]) for i in range(2)]
        vv = [loc(f"v{i}", [P, NG, NT, HD]) for i in range(2)]
        spare = ymem[:, :, :].rearrange("p i c -> p (i c)")
        probs = [loc("probs", [P, 768]), spare[:, 0:768]]
        probsT = [loc("probsT", [P, 768]), spare[:, 768:1536]]
        sq = loc("sq", [P, NT, 2, HD])
        trig = loc("trig", [P, 2, NT, HALF])
        rt = loc("rt", [P, 4, NT, 2, HALF])
        gT = loc("gT", [P, 2, NG])
        ga = loc("ga", [P, 2, NG, ROT])
        load(gT[:, :, :], A["gain_a_cols"].rearrange("p (a g) -> p a g", g=NG), s_misc[2])
        with contextlib.ExitStack() as s0:
            pi = sb_in(s0, "r_pi", [P, NT], I32)
            pf = sb_in(s0, "r_pf", [P, NT])
            inv = sb_in(s0, "r_inv", [P, HALF])
            kk = rt[:, 0, :, 0, :]
            load(pi[:, :], A["positions"][0].rearrange("(i r) -> i r", r=RES), s_misc[2])
            load(inv[:, :], A["inv_freq"], s_misc[2])
            load(ga[:, 0, :, :], A["q_gain_a"][:, :, 0:ROT].to_broadcast([P, NG, ROT]), s_misc[2])
            tl = load(ga[:, 1, :, :], A["k_gain_a"][:, :, 0:ROT].to_broadcast([P, NG, ROT]), s_misc[2])
            t_pos = tl
            arrived = []
            for r in range(RES):
                stage_ = probs[r % 2] if r < 2 else probsT[r % 2]
                tl = load(stage_[:, :], A["mask_a"][:, r * 768:(r + 1) * 768], s_bias[r % 2] if r < 2 else s_misc[5 + r % 2])
                arrived.append((stage_, tl))
            t = dve(lambda e: e.tensor_copy(pf[:, :], pi[:, :]), t_pos)
            a0, a1 = trig[:, 0], trig[:, 1]
            t = dve(lambda e: e.tensor_tensor(a1, pf[:, :].unsqueeze(2).to_broadcast([P, NT, HALF]),
                                              inv[:, :].unsqueeze(1).to_broadcast([P, NT, HALF]), ALU.mult), t)
            magic = 12582912.0
            t = dve(lambda e: e.tensor_scalar(kk, a1, 1.0 / (2 * math.pi), magic, ALU.mult, ALU.add), t)
            t = dve(lambda e: e.tensor_scalar(kk, kk, magic, None, ALU.subtract), t)
            c1 = 6.28125
            c2 = math.floor((2 * math.pi - c1) * 2 ** 20) / 2 ** 20
            c3 = 2 * math.pi - c1 - c2
            for cpart in (c1, c2, c3):
                t = dve(lambda e: e.scalar_tensor_tensor(a1, kk, -cpart, a1, ALU.mult, ALU.add), t)
            t = dve(lambda e: e.tensor_scalar(a0, a1, math.pi / 2, None, ALU.add), t)
            t = dve(lambda e: e.tensor_scalar(kk, a0, math.pi, -2 * math.pi, ALU.is_gt, ALU.mult), t)
            t = dve(lambda e: e.tensor_tensor(a0, a0, kk, ALU.add), t)
            t = dve(lambda e: e.tensor_scalar(trig[:, :, :, :], trig[:, :, :, :], 3.1415925, -3.1415925, ALU.min, ALU.max), t)
            t_rope = act(lambda e: e.activation(trig[:, :, :, :], trig[:, :, :, :], ACT.Sin), t)
        split_piece()
        split_piece()
        yield
        for r, (stage_, tl) in enumerate(arrived):
            t_mask = dve(lambda e: e.tensor_copy(masks[:, r, :], stage_[:, :]), tl)
        free["masks"] = [t_mask, free["const"]]
        for key in (("probs", 0), ("probs", 1), ("probsT", 0), ("probsT", 1)):
            free[key] = t_mask

        def project(h):
            b = h % 2
            for g in range(NG):
                n, wh, wl, ready = next_slab("a")
                slot = (h * NG + g) % 2
                raw_ = qk_raw[slot]
                for i in range(NT):
                    def evacuate(ps, t):
                        act(lambda e: e.activation(raw_[:, i, :, :].rearrange("p a d -> p (a d)"), ps[:, 0:256], ACT.Copy), t, free.get(("qk_raw", slot)))
                        return act(lambda e: e.activation(vv[b][:, g, i, :], ps[:, 256:384], ACT.Copy), t, free.get(("head", b)))
                    ts = slice(i * P, (i + 1) * P)
                    t = yield from product(lambda k: (hx_hi[:, k, ts], hx_lo[:, k, ts]), lambda k: (wh[:, k, :], wl[:, k, :]), KD, slice(0, 384), evacuate, ready, free["hx"],
                                           at=((), (KD - 1,), (3,), ())[i])
                    ada_chunk()
                    yield
                    pump()
                slab_done(n, t)
                rotate_a(h, g, slot, act.last())
                yield

        def rotate_a(h, g, slot, ready):
            b = h % 2
            v8 = qk_raw[slot][:, :, :, :].rearrange("p i a d -> p (i a) d")
            t = head_norms(v8, 2 * NT, HD, sq[:, :, :, :].rearrange("p i a d -> p (i a) d"), ready, free.get("sq"))
            free["sq"] = t
            v32 = qk_raw[slot][:, :, :, 0:ROT]
            t = dve(lambda e: e.tensor_tensor(v32, v32, ga[:, :, g, :].unsqueeze(1).to_broadcast([P, NT, 2, ROT]), ALU.mult), t)
            x1, x2 = v32[:, :, :, 0:HALF], v32[:, :, :, HALF:ROT]
            cos_, sin_ = (trig[:, n].unsqueeze(2).to_broadcast([P, NT, 2, HALF]) for n in range(2))
            for n, (src, tab) in enumerate(((x1, cos_), (x2, sin_), (x2, cos_), (x1, sin_))):
                t1 = dve(lambda e: e.tensor_tensor(rt[:, n], src, tab, ALU.mult), t, t_rope)
            dve(lambda e: e.tensor_tensor(x1, rt[:, 0], rt[:, 1], ALU.subtract), t1)
            tf = dve(lambda e: e.tensor_tensor(x2, rt[:, 2], rt[:, 3], ALU.add), t1)
            hf = free.get(("head", b))
            raw_ = qk_raw[slot]
            to_T(lambda i: raw_[:, i, 0, :], NT, qT[b][:, g, :], gT[:, 0, g:g + 1], lambda: [tf, hf])

            def done(toks):
                free[("qk_raw", slot)] = toks[0]
                free[("qk", b, g)] = toks[1]
            to_T(lambda i: raw_[:, i, 1, :], NT, kT[b][:, g, :], gT[:, 1, g:g + 1], lambda: [tf, hf], done)

        def head_units(h):
            b = h % 2
            units = []
            for r in range(RES):
                segs = [(qT[b][:, 0, r * P:(r + 1) * P], kT[b][:, 0, :], 0, 512)]
                segs += [(qT[b][:, g, r * P:(r + 1) * P], kT[b][:, g, r * P:(r + 1) * P], 384 + g * P, P) for g in (1, 2)]
                values = [vv[b][:, 0, j, :] for j in range(NT)] + [vv[b][:, g, r, :] for g in (1, 2)]
                units.append(group_unit(b, r, segs, values, y[:, r, h * HD:(h + 1) * HD]))
            return units

        def group_unit(b, r, segs, values, dst):
            def softmax(u):
                u.stats = stats(4)
                mx, nm, den, rden = (u.stats[:, i:i + 1] for i in range(4))
                sc, sb_, sfree = take_scores()
                for qq, kk_, c, w in segs:
                    pe(lambda e: e.matmul(sc[:, c:c + w], qq, kk_, start=True, stop=False),
                       *sfree, *[free[("qk", b, g)] for g in range(NG)], signal=False)
                    t = pe(lambda e: e.matmul(sc[:, c:c + w], identb[:, :], masks[:, r, c:c + w], start=False, stop=True), free["masks"])
                yield
                t = dve(lambda e: e.reduce_max(mx, sc[:, 0:768], AX.X), t)
                t = dve(lambda e: e.tensor_scalar(nm, mx, -(HD ** -0.5), None, ALU.mult), t)
                t = act(lambda e: e.activation(u.probs[:, 0:768], sc[:, 0:768], ACT.Exp, bias=nm, scale=HD ** -0.5, accum_out=den), t, free.get(("probs", u.slot)))
                scores_read(sb_, t)
                u.ready = t

            def finish(u, o, t):
                mx, nm, den, rden = (u.stats[:, i:i + 1] for i in range(4))
                td = dve(lambda e: e.reciprocal(rden, den), u.ready)
                return act(lambda e: e.activation(dst, o, ACT.Copy, scale=rden), t, td)
            return Unit(softmax, 768, values, HD, finish)

        for _ in project(0):
            pass
        for h in range(AH):
            main = project(h + 1) if h + 1 < AH else iter(())
            for _ in range(LEAD):
                next(main, None)
            flush()
            weave(main, 3 * (NT * (KD + 1) + 1) - LEAD, pipeline(head_units(h), probs, probsT), 14)
            free[("head", h % 2)] = pe.last()
        flush()
        fence()
        st.close()

    def gated_heads(y):
        fence()
        st = contextlib.ExitStack()
        loc = lambda n, shape, dt=F32: sb_in(st, f"b_{n}", shape, dt)
        carry = loc("carry", [P, S])
        lmask = loc("lmask", [P, 8, P])
        og = loc("og", [P, HD])
        lb = loc("lb", [P, 4, AH])
        qT = [loc(f"qT{i}", [P, S]) for i in range(2)]
        kT = [loc(f"kT{i}", [P, S]) for i in range(2)]
        G = [loc(f"G{i}", [P, S]) for i in range(2)]
        vT = loc("vT", [P, S])
        vN = [loc(f"vN{i}", [P, NT, HD]) for i in range(2)]
        masked = [loc(f"masked{i}", [P, NT, P]) for i in range(2)]
        w2 = loc("w2", [P, S])
        E = [loc(f"E{i}", [P, S]) for i in range(2)]
        qd = [loc(f"qd{i}", [P, S]) for i in range(3)]
        kd = [loc(f"kd{i}", [P, S]) for i in range(3)]
        lnb = loc("lnb", [P, S])
        inv = loc("inv", [P, S])
        attn = loc("attn", [P, NT, P])
        kdN = loc("kdN", [P, NT - 1, P])
        state = loc("state", [P, NT - 1, HD])
        load(carry[:, :], A["carry"], s_misc[3], free["stage"])
        load(lmask[:, :, :], A["level_mask"].rearrange("p (l t) -> p l t", l=8), s_misc[3])
        load(og[:, :], A["o_gain_b"].to_broadcast([P, HD]), s_misc[3])
        tl = load(lb[:, 0:2, :], A["lb_cols"].rearrange("p (n k) -> p n k", k=AH), s_misc[3])
        l0, l1, l2, l3 = (lb[:, i, :] for i in range(4))
        t = dve(lambda e: e.tensor_tensor(l2, l0, l1, ALU.max), tl)
        t = dve(lambda e: e.tensor_tensor(l0, l0, l2, ALU.subtract), t)
        t = dve(lambda e: e.tensor_tensor(l1, l1, l2, ALU.subtract), t)
        t = act(lambda e: e.activation(lb[:, 0:2, :], lb[:, 0:2, :], ACT.Exp), t)
        t = dve(lambda e: e.tensor_tensor(l2, l0, l1, ALU.add), t)
        t = dve(lambda e: e.reciprocal(l2, l2), t)
        t = dve(lambda e: e.tensor_tensor(l1, l1, l2, ALU.mult), t)
        t_lb = dve(lambda e: e.tensor_scalar(l3, l1, -1.0, 1.0, ALU.mult, ALU.add), t)

        def project(h):
            b = h % 2
            n, wh, wl, ready = next_slab("b")
            lbc, omc = lb[:, 1, h:h + 1], lb[:, 3, h:h + 1]
            hb = free.get(("head", b))

            def keep_q(ps, t):
                free[("q", b)] = act(lambda e: e.activation(qT[b][:, :], ps[:, :], ACT.Copy), t, hb)
                return free[("q", b)]

            def decays(ps, t):
                ee, rr = kT[b][:, :], G[b][:, :]
                t0 = dve(lambda e: e.tensor_scalar(ee, ps[:, :], -44.0, None, ALU.max), t, hb)
                chain.append(lambda t: act(lambda e: e.activation(ee, ee, ACT.Exp, scale=-1.0), t0))
                chain.append(lambda t: act(lambda e: e.activation(rr, ee, ACT.Ln, bias=ones[:, 0:1]), t, free["ones"]))
                chain.append(lambda t: act(lambda e: e.activation(lnb[:, :], ee, ACT.Ln, scale=lbc, bias=ones[:, 0:1]), t, t_lb))
                chain.append(lambda t: act(lambda e: e.activation(inv[:, :], rr, ACT.Exp, scale=-1.0), t))
                chain.append(lambda t: dve(lambda e: e.tensor_tensor(rr, lnb[:, :], rr, ALU.subtract), t))
                chain.append(lambda t: dve(lambda e: e.tensor_tensor_scan(rr, carry[:, :], rr, 0.0, ALU.mult, ALU.add), t))
                chain.append(lambda t: dve(lambda e: e.scalar_tensor_tensor(ee, ee, omc, inv[:, :], ALU.mult, ALU.mult), t))
                return t0

            def keep_v(ps, t):
                t1 = act(lambda e: e.activation(vT[:, :], ps[:, :], ACT.Copy), t, free.get("vT"))

                def done(toks):
                    free["vT"], free[("v", b)] = toks
                to_T(lambda i: vT[:, i * P:(i + 1) * P], NT, vN[b][:, :, :].rearrange("p i d -> p (i d)"), None, lambda: [t1, hb], done)
                return t1

            chain, link = [], None
            for part, evacuate in ((1, decays), (2, keep_v), (0, keep_q)):
                cs = slice(part * P, (part + 1) * P)
                steps = product(lambda k: (wh[:, k, cs], wl[:, k, cs]), lambda k: (hx_hi[:, k, :], hx_lo[:, k, :]), KD, slice(0, S), evacuate, ready, free["hx"],
                                at=(3,) if part == 0 else ())
                for _ in steps:
                    yield
                    if chain:
                        link = free[("kg", b)] = chain.pop(0)(link)
                pump()
            flush()
            slab_done(n, pe.last())

        def scan(h):
            b = h % 2
            kg = [free[("kg", b)], free[("q", b)]]
            chunked = lambda ap: ap.rearrange("p (c t) -> p c t", t=CHUNK)
            n_levels = len(LEVELS) + 1

            def decayed(n):
                L = LEVELS[n]
                pairs = lambda ap: ap.rearrange("p (m two l) -> p m two l", two=2, l=L)
                En = E[n % 2]
                g4, e4 = pairs(G[b][:, :]), pairs(En[:, :])
                ref = g4[:, :, 0, L - 1:L].to_broadcast([P, S // (2 * L), L])
                dve(lambda e: e.tensor_tensor(e4[:, :, 0, :], ref, g4[:, :, 0, :], ALU.subtract), kg, free.get(("E", n % 2)))
                t1 = dve(lambda e: e.tensor_tensor(e4[:, :, 1, :], g4[:, :, 1, :], ref, ALU.subtract), kg)
                return act(lambda e: e.activation(En[:, :], En[:, :], ACT.Exp), t1)

            def scaled(n, t1):
                j = n % 3
                tq = dve(lambda e: e.tensor_tensor(qd[j][:, :], qT[b][:, :], E[n % 2][:, :], ALU.mult), t1, kg, free.get(("qd", j)))
                tk = pool(lambda e: e.tensor_tensor(kd[j][:, :], kT[b][:, :], E[n % 2][:, :], ALU.mult), t1, kg, free.get(("qd", j)))
                free[("E", n % 2)] = [tq, tk]
                return [tq, tk]

            def masked_sum(n, bank, t):
                mk = lmask[:, n, :].unsqueeze(1).to_broadcast([P, NT, P])
                src = banks[bank].rearrange("p (c t) -> p c t", t=P)
                if n == 0:
                    t1 = dve(lambda e: e.tensor_tensor(attn[:, :, :], src, mk, ALU.mult), t, free.get("attn"))
                    free[bank] = free["attn sum"] = t1
                    return t1
                m = masked[n % 2]
                t1 = dve(lambda e: e.tensor_tensor(m[:, :, :], src, mk, ALU.mult), t, free.get(("masked", n % 2)))
                free[bank] = t1
                t2 = pool(lambda e: e.tensor_tensor(attn[:, :, :], attn[:, :, :], m[:, :, :], ALU.add), t1, free["attn sum"])
                free[("masked", n % 2)] = free["attn sum"] = t2
                return t2

            def level_product(n, ready):
                bank = 2 + n % 4
                q_, k_ = (qd[n % 3], kd[n % 3]) if n < len(LEVELS) else (qT[b], kT[b])
                for c in range(NT):
                    cs = slice(c * P, (c + 1) * P)
                    t = pe(lambda e: e.matmul(banks[bank][:, cs], k_[:, cs], q_[:, cs], start=True, stop=True), ready, free.get(bank), signal=(c == NT - 1))
                if n < len(LEVELS):
                    free[("qd", n % 3)] = t
                return bank, t

            t1 = decayed(0)
            t_next = decayed(1)
            ready = scaled(0, t1)
            yield
            made = []
            for n in range(n_levels):
                ready_next = None
                if n + 1 < len(LEVELS):
                    ready_next = scaled(n + 1, t_next)
                if n + 2 < len(LEVELS):
                    t_next = decayed(n + 2)
                if n + 1 == len(LEVELS):
                    te = act(lambda e: e.activation(E[1][:, :], G[b][:, :], ACT.Exp), kg, free.get(("E", 1)))
                    t3 = dve(lambda e: e.tensor_tensor(chunked(w2[:, :]), chunked(G[b][:, :])[:, :, P - 1:P].to_broadcast([P, NT, P]),
                                                       chunked(G[b][:, :]), ALU.subtract), kg, free.get("w2"))
                    t3 = act(lambda e: e.activation(w2[:, :], w2[:, :], ACT.Exp), t3)
                yield
                bank, tp = level_product(n, ready)
                yield
                if made:
                    ta = masked_sum(*made.pop())
                if ready_next:
                    ready = ready_next
                elif n + 1 == len(LEVELS):
                    glast = stats(NT)
                    xj = (n + 1) % 3
                    t2 = dve(lambda e: e.tensor_copy(glast, chunked(E[1][:, :])[:, :, P - 1]), te)
                    tq = dve(lambda e: e.tensor_tensor(qd[xj][:, :], qT[b][:, :], E[1][:, :], ALU.mult), te, kg, free.get(("qd", xj)))
                    tkd = dve(lambda e: e.tensor_tensor(kd[xj][:, :], kT[b][:, :], w2[:, :], ALU.mult), t3, kg, free.get(("qd", xj)))
                    free[("E", 1)] = [tq, t2]
                    free["w2"] = tkd
                    ready = kg
                made.append((n, bank, tp))
            for i in range(NT - 1):
                cs = slice(i * P, (i + 1) * P)
                tt = pe(lambda e: e.transpose(tr_ps[:, cs], kd[xj][:, cs], ident[:, :]), tkd, free.get(6), signal=(i == NT - 2))
            free[6] = tn = act(lambda e: e.activation(kdN[:, :, :].rearrange("p i d -> p (i d)"), tr_ps[:, 0:(NT - 1) * P], ACT.Copy), tt, free.get("kdN"))
            ta = masked_sum(*made.pop())
            yield
            bank = 2
            for c in range(NT - 1):
                ts = pe(lambda e: e.matmul(banks[bank][:, c * P:(c + 1) * P], kdN[:, c, :], vN[b][:, c, :], start=True, stop=True),
                        tn, free[("v", b)], free.get(bank), signal=(c == NT - 2))
            free["kdN"] = ts
            t = dve(lambda e: e.tensor_copy(state[:, 0, :], banks[bank][:, 0:HD]), ts, free.get("state"))
            for c in range(1, NT - 1):
                t = dve(lambda e: e.scalar_tensor_tensor(state[:, c, :], state[:, c - 1, :], glast[:, c:c + 1], banks[bank][:, c * P:(c + 1) * P],
                                                         ALU.mult, ALU.add), t, t2)
            free[bank] = tstate = t
            yield
            yield
            for c in range(NT):
                cs = slice(c * P, (c + 1) * P)
                t = pe(lambda e: e.matmul(out_ps[:, cs], attn[:, c, :], vN[b][:, c, :], start=True, stop=(c == 0)), ta, free[("v", b)], free.get(7))
                if c:
                    t = pe(lambda e: e.matmul(out_ps[:, cs], qd[xj][:, cs], state[:, c - 1, :], start=False, stop=True), tq, tstate)
            free["attn"] = free["state"] = free[("head", b)] = free[("qd", xj)] = t
            yv = y[:, :, h * HD:(h + 1) * HD]
            free[7] = to = act(lambda e: e.activation(yv, out_ps[:, :].rearrange("p (c d) -> p c d", d=HD), ACT.Copy), t)
            yield
            t = head_norms(yv, NT, HD, w2[:, :].rearrange("p (i d) -> p i d", d=HD), to, free["w2"], eng=pool)
            free["w2"] = t
            pool(lambda e: e.tensor_tensor(yv, yv, og[:, :].unsqueeze(1).to_broadcast([P, NT, HD]), ALU.mult), t)
            yield

        for _ in project(0):
            pass
        for h in range(AH):
            weave(project(h + 1) if h + 1 < AH else iter(()), 3 * KD, scan(h), 30)
        fence()
        st.close()
        yield

    def second_block():
        ctxs = contextlib.ExitStack()
        keep = lambda n, shape, dt=F32: sb_in(ctxs, f"s_{n}", shape, dt)
        cx = keep("ctx", [P, NC, D])
        hc_hi = keep("hc_hi", [P, KD, CTX], F32R)
        hc_lo = keep("hc_lo", [P, KD, CTX], F32R)
        g2 = keep("g2", [P, 2, 2, KD])
        amp = keep("amp", [P, 2, 2, KD, 2])
        cos2 = keep("cos2", [P, NT, HD2])
        sin2 = keep("sin2", [P, NT, HD2])
        c_hi, c_lo = (lambda k: hc_hi[:, k, :]), (lambda k: hc_lo[:, k, :])
        load(g2[:, :, :, :], A["gain_cols_2"].rearrange("p (l a k) -> p l a k", l=2, a=2), s_misc[4], free["stage"])
        load(cos2[:, :, :], A["cos2"].rearrange("(i p) c -> p i c", p=P), s_misc[4])
        load(sin2[:, :, :], A["sin2"].rearrange("(i p) c -> p i c", p=P), s_misc[4])
        t_in = load(cx[:, :, :], A["ctx_2"][0].rearrange("(i p) d -> p i d", p=P), s_misc[4])
        for layer in range(2):
            for a in range(2):
                for c in range(2):
                    t = dve(lambda e: e.scalar_tensor_tensor(amp[:, layer, a, :, c], mod[:, layer, 3 * a + 1, :, c], 1.0, g2[:, layer, a, :], ALU.add, ALU.mult),
                            t_in, free["mod"])
        free["cols"] = t

        x_tiles = [((lambda k, i=i: hx_hi[:, k, i * P:(i + 1) * P]), (lambda k, i=i: hx_lo[:, k, i * P:(i + 1) * P])) for i in range(NT)]
        c_tiles = [((lambda k, i=i: hc_hi[:, k, i * P:(i + 1) * P]), (lambda k, i=i: hc_lo[:, k, i * P:(i + 1) * P])) for i in range(NC)]

        def mod_row(layer, which, c, dst, diag, *after):
            for half in range(2):
                bank, key = take_wide()
                for k in range(4):
                    kk = half * 4 + k
                    td = dve(lambda e: e.tensor_scalar(diag[:, k % 2, :], ident[:, :], mod[:, layer, which, kk, c:c + 1], None, ALU.mult),
                             free.get(("diag", k % 2)), *after)
                    tp = pe(lambda e: e.matmul(bank[:, k * P:(k + 1) * P], ones[:, :], diag[:, k % 2, :], start=True, stop=True), td, free.get(key))
                    free[("diag", k % 2)] = tp
                t = act(lambda e: e.activation(dst[:, half * 512:(half + 1) * 512], bank[:, :], ACT.Copy), tp)
                free[key] = t
            return t

        def norm_all(layer, a, with_ctx, y):
            amp_, shift = (lambda k, c: amp[:, layer, a, k, c:c + 1]), (lambda k, c: mod[:, layer, 3 * a, k, c:c + 1])
            t = normed_to_T(x, NT, y[:, 0:NT, :], lambda k: amp_(k, 0), lambda k: shift(k, 0), x_hi, x_lo, False)
            if with_ctx:
                scr, after = (y[:, NT:NT + NC, :], None) if layer == 0 else (y[:, 0:NC, :], free["scratch"])
                t = normed_to_T(cx, NC, scr, lambda k: amp_(k, 1), lambda k: shift(k, 1), c_hi, c_lo, False, after)
            return t

        def rotate(v3, i, nheads, tmp, *after):
            v = v3.rearrange("p h (a b c) -> p h a b c", a=2, b=2)
            t3 = tmp[:, 0:nheads * HD2].rearrange("p (h c) -> p h c", c=HD2)
            w = t3.rearrange("p h (a b c) -> p h a b c", a=2, b=2)
            sv = sin2[:, i, :].rearrange("p (a b c) -> p a b c", a=2, b=2)
            for b in range(2):
                t = dve(lambda e: e.tensor_tensor(w[:, :, :, b, :], v[:, :, :, 1 - b, :],
                                                  sv[:, :, b, :].unsqueeze(1).to_broadcast([P, nheads, 2, 16]), ALU.mult), *after, free.get("rot"))
            t = dve(lambda e: e.tensor_tensor(v3, v3, cos2[:, i, :].unsqueeze(1).to_broadcast([P, nheads, HD2]), ALU.mult), t)
            free["rot"] = dve(lambda e: e.tensor_tensor(v3, v3, t3, ALU.add), t)
            return free["rot"]

        def turn_tile(ring, slot, blocks, dst, done, *after):
            def go():
                bank, key = idle_proj()
                for m in blocks:
                    c = (m - blocks[0]) * P
                    tp = pe(lambda e: e.transpose(bank[:, c:c + P], ring[:, slot, m * P:(m + 1) * P], ident[:, :]),
                            free.get(key), *after, signal=(m == blocks[-1]))
                free[("ring", slot)] = tp
                src = bank[:, 0:len(blocks) * P].rearrange("p (m t) -> p m t", t=P)
                free[key] = act(lambda e: e.activation(dst, src, ACT.Copy), tp, *after)
                done(free[key])
            pending.append(go)

        NTC = NT + NC
        RING = 3

        def run_heads(count, project, units, probs, probsT, n_steps):
            for _ in project(0):
                pass
            for u in range(count):
                main = project(u + 1) if u + 1 < count else iter(())
                for _ in range(KD - 1):
                    next(main, None)
                flush()
                weave(main, NTC * KD - (KD - 1), pipeline(units(u), probs, probsT), n_steps(u))
                free[("head", u % 2)] = pe.last()

        def mix_ab(y):
            st = contextlib.ExitStack()
            loc = lambda n, shape, dt=F32: sb_in(st, f"ab_{n}", shape, dt)
            ring = loc("ring", [P, RING, 2 * HD])
            vN = [loc(f"v{i}", [P, NTC, HD]) for i in range(2)]
            qkT = [loc(f"qkT{i}", [P, 2, NTC * P]) for i in range(2)]
            probs = [loc(f"probs{i}", [P, NTC * P]) for i in range(2)]
            probsT = [loc(f"probsT{i}", [P, NTC * P]) for i in range(2)]
            second = loc("second", [P, 14 * GRID_W])
            norm_scratch = second[:, 0:NTC * HD].rearrange("p (i c) -> p i c", c=HD)
            tmp = loc("tmp", [P, 2 * HD])
            lamv = tmp[:, :].rearrange("p (a c) -> p a c", a=4)
            lam = loc("lam", [P, 4])
            subg = loc("subg", [P, HD])
            lam_init = 0.8 - 0.6 * math.exp(-0.3 * 0)
            load(subg[:, :], A["diff_sub_g_2"].to_broadcast([P, HD]), s_misc[5], free["stage"])
            tl = load(lamv, A["diff_lambda_2"].to_broadcast([P, 4, HD2]), s_misc[5])
            t = dve(lambda e: e.tensor_tensor(lamv[:, 0:4:2, :], lamv[:, 0:4:2, :], lamv[:, 1:4:2, :], ALU.mult), tl)
            t = dve(lambda e: e.tensor_reduce(lam[:, 0:2], lamv[:, 0:4:2, :], AX.X, ALU.add), t)
            t = act(lambda e: e.activation(lam[:, 0:2], lam[:, 0:2], ACT.Exp), t)
            t = dve(lambda e: e.tensor_tensor(lam[:, 2:3], lam[:, 1:2], lam[:, 0:1], ALU.subtract), t)
            t = dve(lambda e: e.tensor_scalar(lam[:, 2:3], lam[:, 2:3], -lam_init, None, ALU.add), t)
            t_lam = free["rot"] = dve(lambda e: e.tensor_scalar(subg[:, :], subg[:, :], 1.0 - lam_init, None, ALU.mult), t)

            def project(u):
                b = u % 2
                n, wh, wl, ready = next_slab("ab")
                for i, (ah, al) in enumerate(x_tiles + c_tiles):
                    slot = i % RING

                    def evacuate(ps, t):
                        t1 = act(lambda e: e.activation(ring[:, slot, :], ps[:, 0:256], ACT.Copy), t, free.get(("ring", slot)))
                        tv = act(lambda e: e.activation(vN[b][:, i, :], ps[:, 256:384], ACT.Copy), t, free.get(("head", b)))
                        if u < 4 and i < NT:
                            t1 = rotate(ring[:, slot, :].rearrange("p (h c) -> p h c", c=HD2), i, 4, tmp, t1)

                        def done(token):
                            free[("qk", b)] = token
                        turn_tile(ring, slot, (0, 1), qkT[b][:, :, i * P:(i + 1) * P], done, t1, free.get(("head", b)))
                        return tv
                    t = yield from product(lambda k: (ah(k), al(k)), lambda k: (wh[:, k, :], wl[:, k, :]), KD, slice(0, 384), evacuate, ready, at=(KD - 2,))
                    pump()
                slab_done(n, t)

            def diff_unit(u, i):
                b = u % 2
                k0, n = (0, NTC * P) if i < NT else (S, CTX)

                def softmax(q):
                    if u and i == 1:
                        sub_norm(u - 1)
                    q.stats = stats(8)
                    maps = []
                    for a in range(2):
                        rows = slice(a * HD2, (a + 1) * HD2)
                        sc, sb_, sfree = take_scores()
                        for c0 in range(0, n, 512):
                            w = min(512, n - c0)
                            t = pe(lambda e: e.matmul(sc[:, c0:c0 + w], qkT[b][rows, 0, i * P:(i + 1) * P], qkT[b][rows, 1, k0 + c0:k0 + c0 + w],
                                                      start=True, stop=True), sfree, free[("qk", b)])
                        maps.append((sc, sb_, t))
                    yield
                    for a, (sc, sb_, t) in enumerate(maps):
                        mx, nm, den, rd = (q.stats[:, 4 * a + m:4 * a + m + 1] for m in range(4))
                        dst, before = (q.probs, free.get(("probs", q.slot))) if a == 0 else (second, free.get("second"))
                        t = dve(lambda e: e.reduce_max(mx, sc[:, 0:n], AX.X), t)
                        t = dve(lambda e: e.tensor_scalar(nm, mx, -(HD2 ** -0.5), None, ALU.mult), t)
                        t = act(lambda e: e.activation(dst[:, 0:n], sc[:, 0:n], ACT.Exp, bias=nm, scale=HD2 ** -0.5, accum_out=den), t, before)
                        scores_read(sb_, t)
                    d0, d1, r1 = q.stats[:, 2:3], q.stats[:, 6:7], q.stats[:, 7:8]
                    t = dve(lambda e: e.reciprocal(r1, d1), t)
                    t = dve(lambda e: e.tensor_scalar(r1, r1, d0, lam[:, 2:3], ALU.mult, ALU.mult), t, t_lam)
                    q.ready = free["second"] = dve(lambda e: e.scalar_tensor_tensor(q.probs[:, 0:n], second[:, 0:n], r1, q.probs[:, 0:n], ALU.mult, ALU.add), t)

                def finish(q, o, t):
                    r0 = q.stats[:, 3:4]
                    td = dve(lambda e: e.reciprocal(r0, q.stats[:, 2:3]), q.ready)
                    dst = y[:, i, u * HD:(u + 1) * HD]
                    free["diff out"] = act(lambda e: e.activation(dst, o, ACT.Copy, scale=r0), t, td)
                    return free["diff out"]
                return Unit(softmax, n, [vN[b][:, k0 // P + j, :] for j in range(n // P)], HD, finish)

            def sub_norm(u):
                yv = y[:, :, u * HD:(u + 1) * HD]
                t = free["second"] = head_norms(yv, NTC, HD, norm_scratch, free["diff out"], free["second"])
                dve(lambda e: e.tensor_tensor(yv, yv, subg[:, :].unsqueeze(1).to_broadcast([P, NTC, HD]), ALU.mult), t, t_lam)

            def load_bias(head):
                free["table"] = load(second[:, :], A["bias_tab"][head].rearrange("p j c -> p (j c)"), s_bias[0], free["second"], free.get("bias"))

            def neighbour_unit(u, a, i):
                b, head = u % 2, (u - 4) * 2 + a
                rows = slice(a * HD2, (a + 1) * HD2)
                q = qkT[b][rows, 0, i * P:(i + 1) * P]
                dst = y[:, i, DIFF_W + head * HD2:DIFF_W + (head + 1) * HD2]
                ready = lambda: [free[("qk", b)]]
                if i < NT:
                    segs = [(qkT[b][rows, 1, 0:S], 0, S, None), (qkT[b][rows, 1, S:S + CTX], S, CTX, None)]
                    o = (6 - 2 * i) * GRID_W
                    return plain_unit(q, segs, NTC * P, [vN[b][:, j, rows] for j in range(NTC)], HD2, HD2 ** -0.5, dst,
                                      bias=lambda: (second[:, o:o + S], free["table"]), after=ready)

                def ready_then_load():
                    if i == NT and head < 7:
                        load_bias(head + 1)
                    return ready()
                return plain_unit(q, [(qkT[b][rows, 1, S:S + CTX], 0, CTX, None)], CTX, [vN[b][:, j, rows] for j in range(NT, NTC)],
                                  HD2, HD2 ** -0.5, dst, after=ready_then_load)

            def units(u):
                if u < 4:
                    return [diff_unit(u, i) for i in range(NTC)]
                if u == 4:
                    sub_norm(3)
                    load_bias(0)
                return [neighbour_unit(u, a, i) for a in range(2) for i in range(NTC)]

            run_heads(8, project, units, probs, probsT, lambda u: 15 if u < 4 else 33)
            fence()
            st.close()

        def mix_c(y):
            st = contextlib.ExitStack()
            loc = lambda n, shape, dt=F32: sb_in(st, f"c_{n}", shape, dt)
            band = loc("band", [P, 2, P], BF16)
            sinks = loc("sinks", [P, 16])
            ring = loc("ring", [P, RING, 384])
            vN = [loc(f"v{i}", [P, NTC, HD2]) for i in range(2)]
            qT = [loc(f"qT{i}", [P, 3, NTC * P]) for i in range(2)]
            probs = [loc(f"probs{i}", [P, 5 * P]) for i in range(2)]
            probsT = [loc(f"probsT{i}", [P, 5 * P]) for i in range(2)]
            tmp = loc("tmp", [P, 384])
            bandf = tmp[:, 0:2 * P]
            load(sinks[:, :], A["attn_sinks_2"].to_broadcast([P, 16]), s_misc[6], free["stage"])
            tl = load(bandf, A["band"], s_misc[6])
            t = free["rot"] = dve(lambda e: e.tensor_copy(band[:, :, :].rearrange("p a k -> p (a k)"), bandf), tl)
            free["masks"] = [t, free["const"]]

            def project(j):
                b = j % 2
                n, wh, wl, ready = next_slab("c")
                for i, (ah, al) in enumerate(x_tiles + c_tiles):
                    slot, c0 = i % RING, 0 if i < NT else 256

                    def evacuate(ps, t):
                        before = free.get(("ring", slot))
                        if i < NT:
                            act(lambda e: e.activation(ring[:, slot, 0:256], ps[:, 0:256], ACT.Copy), t, before)
                        t1 = act(lambda e: e.activation(ring[:, slot, 256:384].rearrange("p (a c) -> p a c", a=2),
                                                        ps[:, 256:320].unsqueeze(1).to_broadcast([P, 2, HD2]), ACT.Copy), t, before)
                        tv = act(lambda e: e.activation(vN[b][:, i, :], ps[:, 320:384], ACT.Copy), t, free.get(("head", b)))
                        if i < NT:
                            t1 = rotate(ring[:, slot, :].rearrange("p (h c) -> p h c", c=HD2), i, 6, tmp, t1)

                        def done(token):
                            free[("qk", b)] = token
                        blocks = (0, 1, 2) if i < NT else (2,)
                        turn_tile(ring, slot, blocks, qT[b][:, blocks[0]:3, i * P:(i + 1) * P], done, t1, free.get(("head", b)))
                        return tv
                    t = yield from product(lambda k: (ah(k), al(k)), lambda k: (wh[:, k, c0:384], wl[:, k, c0:384]), KD, slice(c0, 384), evacuate, ready, at=(KD - 2,))
                    pump()
                slab_done(n, t)

            def window_unit(j, hh, i):
                b, head = j % 2, j * 4 + hh
                a, part = hh // 2, hh % 2
                rows = slice(part * HD2, (part + 1) * HD2)
                blocks = [m for m in (i - 1, i, i + 1) if 0 <= m < NT] + [NT, NT + 1]
                segs = []
                for n_, m in enumerate(blocks):
                    mask = None if m >= NT or m == i else band[:, 0 if m < i else 1, :]
                    segs.append((qT[b][rows, 2, m * P:(m + 1) * P], n_ * P, P, mask))
                return plain_unit(qT[b][rows, a, i * P:(i + 1) * P], segs, len(blocks) * P, [vN[b][:, m, :] for m in blocks], HD2, HD2 ** -0.5,
                                  y[:, i, head * HD2:(head + 1) * HD2], sink=sinks[:, head:head + 1], after=lambda: [free[("qk", b)]])

            run_heads(4, project, lambda j: [window_unit(j, hh, i) for hh in range(4) for i in range(NT)], probs, probsT, lambda j: 48)
            fence()
            st.close()

        def tail(layer, y, with_ctx, ls):
            tiles = x_tiles + (c_tiles if with_ctx else [])
            rows_of = lambda i: x[:, i, :] if i < NT else cx[:, i - NT, :]
            st = contextlib.ExitStack()
            loc = lambda n, shape, dt=F32: sb_in(st, f"t{layer}_{n}", shape, dt)
            row = [loc(f"row{c}", [P, D]) for c in range(2 if with_ctx else 1)]
            diag = loc("diag", [P, 2, P])
            gtmp = loc("gtmp", [P, 2, 512])
            rows_to_T(y[:, 0:NT, :], NT, KD, x_hi, x_lo, False)
            if with_ctx:
                rows_to_T(y[:, NT:NT + NC, :], NC, KD, c_hi, c_lo, False)
            th = dve.last()
            trow = [mod_row(layer, 2, c, row[c], diag) for c in range(len(row))]
            fence()
            for c0, c1 in COLS:
                n, wh, wl, ready = next_slab("out2")
                w = c1 - c0
                for i, (ah, al) in enumerate(tiles):
                    ps, key = take_wide()
                    for k in range(KD):
                        t = mm3(ps[:, 0:w], (ah(k), al(k)), (wh[:, k, :], wl[:, k, :]), k == 0, k == KD - 1, ready, free.get(key))
                    pump()
                    free[key] = add_gated(rows_of(i)[:, c0:c1], ps[:, 0:w], row[0 if i < NT else 1][:, c0:c1], gtmp, t)
                slab_done(n, t)
            fence()
            st.close()
            if stage == 3:
                ls.close()
                return
            norm_all(layer, 1, with_ctx, y)
            fence()
            ls.close()
            st = contextlib.ExitStack()
            loc = lambda n, shape, dt=F32: sb_in(st, f"f{layer}_{n}", shape, dt)
            row = [loc(f"row{c}", [P, D]) for c in range(2 if with_ctx else 1)]
            diag = loc("diag", [P, 2, P])
            gtmp = loc("gtmp", [P, 2, 512])
            trow = [mod_row(layer, 5, c, row[c], diag) for c in range(len(row))]
            NTOK = S + (CTX if with_ctx else 0)
            gh = loc("gh", [P, 6, NTOK], F32R)
            gl = loc("gl", [P, 6, NTOK], F32R)
            fence()
            hs = loc("hs", [P, 2, S])
            for a, b in FPARTS:
                for j in range(a, b):
                    n, wh, wl, ready = next_slab("up")
                    for c0, width, hi_of, lo_of in ((0, S, x_hi, x_lo), (S, CTX, c_hi, c_lo))[0:2 if with_ctx else 1]:
                        pair = []
                        for part in range(2):
                            ps, key = take_wide()
                            for k in range(KD):
                                cs_ = slice(part * P, (part + 1) * P)
                                t = mm3(ps[:, 0:width], (wh[:, k, cs_], wl[:, k, cs_]), (hi_of(k), lo_of(k)), k == 0, k == KD - 1, ready, free.get(key))
                            pair.append((ps, key, t))
                            pump()
                        (pa, ka, ta), (pb, kb, tb) = pair
                        slot = turn.setdefault("hs", 0) % 2
                        turn["hs"] += 1
                        h_ = hs[:, slot, 0:width]
                        t1 = act(lambda e: e.activation(h_, pa[:, 0:width], ACT.Silu), ta, free.get(("hs", slot)))
                        free[ka] = t1
                        t1 = dve(lambda e: e.tensor_tensor(h_, h_, pb[:, 0:width], ALU.mult), t1, tb)
                        free[kb] = t1
                        gv = (slice(None), j - a, slice(c0, c0 + width))
                        t2 = act(lambda e: e.activation(gh[gv], h_, ACT.Copy), t1, free.get("gT"))
                        t3 = dve(lambda e: e.tensor_tensor(gl[gv], h_, gh[gv].bitcast(F32), ALU.subtract), t2)
                        free[("hs", slot)] = t3
                    slab_done(n, tb)
                for half in range(2):
                    n, wh, wl, ready = next_slab("down")
                    for i in range(len(tiles)):
                        ps, key = take_wide()
                        for k in range(b - a):
                            gv = (slice(None), k, slice(i * P, (i + 1) * P))
                            t = mm3(ps[:, 0:512], (gh[gv], gl[gv]), (wh[:, k, :], wl[:, k, :]), k == 0, k == b - a - 1, ready, t3, free.get(key))
                        pump()
                        cc = slice(half * 512, (half + 1) * 512)
                        free[key] = add_gated(rows_of(i)[:, cc], ps[:, :], row[0 if i < NT else 1][:, cc], gtmp, t)
                    slab_done(n, t)
                free["gT"] = t
            fence()
            st.close()

        def add_gated(dst, ps, row, gtmp, t):
            slot = turn.setdefault("gadd", 0) % 2
            turn["gadd"] += 1
            w = dst.shape[-1]
            m = gtmp[:, slot, 0:w]
            t = dve(lambda e: e.tensor_tensor(m, ps, row, ALU.mult), t, free.get(("gadd", slot)))
            free[("gadd", slot)] = pool(lambda e: e.tensor_tensor(dst, dst, m, ALU.add), t)
            return t

        for layer in range(2):
            ls = contextlib.ExitStack()
            y = sb_in(ls, f"s{layer}_y", [P, NT + NC if layer == 0 else NT, D])
            norm_all(layer, 0, True, y)
            fence()
            if layer == 0:
                mix_ab(y)
            else:
                mix_c(y)
            tail(layer, y, layer == 0, ls)
            if stage in (3, 4) and layer == 0:
                dump(x[:, :, :])
                ctxs.close()
                return
        with contextlib.ExitStack() as s1:
            fg = sb_in(s1, "fin_g", [P, D])
            o = sb_in(s1, "fin_o", [P, NT, D])
            tg = load(fg[:, :], A["final_g_2"].unsqueeze(0).to_broadcast([P, D]), s_misc[7], free["stage"])
            ss = stats(NT)
            for i in range(NT):
                t = act(lambda e: e.activation(o[:, i, :], x[:, i, :], ACT.Square, accum_out=ss[:, i:i + 1]))
            t = inv_rms(ss, D, t)
            for i in range(NT):
                t2 = dve(lambda e: e.scalar_tensor_tensor(o[:, i, :], x[:, i, :], ss[:, i:i + 1], fg[:, :], ALU.mult, ALU.mult), t, tg)
                load(out[0, i * P:(i + 1) * P, :], o[:, i, :], s_out, t2)
            sp.wait(s_out.token())
        ctxs.close()

    first_block_layer(0)
    if stage == 1:
        dump(x[:, :, :])
    if not finished["v"]:
        first_block_layer(1)
    if stage == 2:
        dump(x[:, :, :])
    first_scope.close()
    if not finished["v"]:
        second_block()

    with nc.Block() as block:
        @block.sync
        def _(e):
            sp.emit(e)

        @block.tensor
        def _(e):
            pe.emit(e)

        @block.scalar
        def _(e):
            act.emit(e)

        @block.vector
        def _(e):
            dve.emit(e)

        @block.gpsimd
        def _(e):
            pool.emit(e)
    ctx.close()


def arrays_of(inputs):
    a = {k: np.ascontiguousarray(v) for k, v in inputs.items()}
    c = dict(shape_constants())
    cols = lambda v: np.ascontiguousarray(np.asarray(v).reshape(-1, KD, P).transpose(2, 0, 1)).reshape(P, -1)
    c["gain_cols"] = np.concatenate([cols(a["norm_gain"]), cols(a["mem_norm_gain"]), cols(a["norm_g_2"][:, 0])], 1)
    c["gain_cols_2"] = cols(a["norm_g_2"])
    c["c_cols"] = np.concatenate([cols(a["c_2"]), cols(a["c_ctx_2"])], 1)
    c["ada_b_cols"] = cols(a["ada_b_2"])
    c["lb_cols"] = cols(a["lb_logits"])
    g = np.concatenate([a["q_gain_a"][0], a["k_gain_a"][0]], 0).T.copy()
    g[:ROT] = 1.0
    c["gain_a_cols"] = g
    c["bias_tab"] = bias_table(a.pop("na_rpb_2")[0])
    a.pop("norm_gain"), a.pop("mem_norm_gain"), a.pop("lb_logits"), a.pop("norm_g_2")
    a.pop("c_2"), a.pop("c_ctx_2"), a.pop("ada_b_2")
    return {**a, **c}


def declare(nc, arrays, stage=99):
    aps = {n: nc.dram_tensor(f"in_{n}", v.shape, mybir.dt.from_np(v.dtype), kind="ExternalInput").ap() for n, v in arrays.items()}
    out = nc.dram_tensor("out", (1, S, D), F32, kind="ExternalOutput").ap()
    build(nc, aps, out, stage)


def kernel(**inputs):
    import concourse.bacc as bacc
    from concourse.bass_utils import run_bass_kernel_spmd
    arrays = arrays_of(inputs)
    nc = bacc.Bacc("TRN2", target_bir_lowering=False, num_devices=1)
    declare(nc, arrays)
    r = run_bass_kernel_spmd(nc, [{f"in_{n}": v for n, v in arrays.items()}], core_ids=[0])
    return r.results[0]["out"]
```
